# Optimizing a Trainium2 kernel written in Bass

```python
import math
import jax
import jax.numpy as jnp
from jax import lax
import numpy as np

D_MODEL = 1024
BATCH = 1
SEQ = 512
DEPTH = 1
DEC_BATCH = 8
DEC_SEQ = 1
PAST_LEN = 1024
PAGE_SIZE = 128

N_META = 16
N_HEADS = 8
HEAD_DIM = 64
ATTN_WIDTH = N_HEADS * HEAD_DIM
N_IDX_HEADS = 8
IDX_DIM = 64
TOPK_MAX = 256
N_BUCKETS = 32
MAX_DISTANCE = 128
POOL_WINDOWS = (2, 4, 8, 16)
POOL_GROUPS = 4
POOL_WIDTH = D_MODEL // 2
POOL_GROUP_DIM = POOL_WIDTH // POOL_GROUPS
POOL_STATE = 15
N_EXPERTS = 32
TOP_EXPERTS = 4
D_EXPERT = D_MODEL
SWIGLU_LIMIT = 7.0
SWIGLU_ALPHA = 1.702
MOE_BLOCK = 64
Q_BLOCK = 128
EPS = 1e-6
SEG_WIDTHS = (ATTN_WIDTH, ATTN_WIDTH, ATTN_WIDTH, N_IDX_HEADS * IDX_DIM, IDX_DIM, N_IDX_HEADS, POOL_WIDTH, D_MODEL, D_MODEL)
IN_WIDTH = sum(SEG_WIDTHS)

kernel_name = 'dsa_pool_moe_hybrid_step'

def rms_norm(x, g):
    xf = x.astype(jnp.float32)
    y = xf * lax.rsqrt(jnp.mean(xf * xf, axis=-1, keepdims=True) + EPS)
    return (y * g.astype(jnp.float32)).astype(x.dtype)

def t5_bucket(dist):
    n = jnp.maximum(dist, 0)
    max_exact = N_BUCKETS // 2
    nf = jnp.maximum(n, 1).astype(jnp.float32)
    large = max_exact + (jnp.log(nf / max_exact) / math.log(MAX_DISTANCE / max_exact) * (N_BUCKETS - max_exact)).astype(jnp.int32)
    large = jnp.minimum(large, N_BUCKETS - 1)
    return jnp.where(n < max_exact, n, large)

def project(h, w_in):
    z = h @ w_in
    points = [int(c) for c in np.cumsum(SEG_WIDTHS)[:-1]]
    q, k, v, qi, ki, wi, p, ga, gb = jnp.split(z, points, axis=-1)
    lead = h.shape[:-1]
    q = q.reshape(*lead, N_HEADS, HEAD_DIM)
    k = k.reshape(*lead, N_HEADS, HEAD_DIM)
    v = v.reshape(*lead, N_HEADS, HEAD_DIM)
    qi = qi.reshape(*lead, N_IDX_HEADS, IDX_DIM)
    return q, k, v, qi, ki, wi, p, ga, gb

def sparse_attend(q, qi, wi, q_pos, k_all, v_all, ki_all, rel_bias, k_sel):
    L = k_all.shape[1]
    k_pos = jnp.arange(L, dtype=jnp.int32)
    dots = jnp.einsum('bqhd,bld->bqhl', qi, ki_all).astype(jnp.float32)
    score = jnp.einsum('bqh,bqhl->bql', wi.astype(jnp.float32), jax.nn.relu(dots))
    causal = k_pos[None, :] <= q_pos[:, None]
    score = jnp.where(causal[None], score, -jnp.inf)
    _, idx = lax.top_k(score, k_sel)
    gather = jax.vmap(lambda rows, i: rows[i])
    kg = gather(k_all, idx)
    vg = gather(v_all, idx)
    dist = q_pos[None, :, None] - idx
    bias = rel_bias[t5_bucket(dist)].astype(jnp.float32)
    logits = jnp.einsum('bqhd,bqkhd->bhqk', q, kg).astype(jnp.float32) * (HEAD_DIM ** -0.5) + jnp.transpose(bias, (0, 3, 1, 2))
    logits = jnp.where((dist >= 0)[:, None], logits, -jnp.inf)
    p = jax.nn.softmax(logits, axis=-1)
    return jnp.einsum('bhqk,bqkhd->bqhd', p.astype(vg.dtype), vg)

def blocked_attention(q, qi, wi, pos0, k_all, v_all, ki_all, rel_bias, k_sel):
    B, Q = q.shape[:2]
    bq = min(Q_BLOCK, Q)
    nb = -(-Q // bq)
    pad = nb * bq - Q

    def blocks(a):
        a = jnp.pad(a, [(0, 0), (0, pad)] + [(0, 0)] * (a.ndim - 2))
        return jnp.swapaxes(a.reshape(B, nb, bq, *a.shape[2:]), 0, 1)

    q_pos = (pos0 + jnp.arange(nb * bq, dtype=jnp.int32)).reshape(nb, bq)

    def one_block(args):
        qb, qib, wib, pb = args
        return sparse_attend(qb, qib, wib, pb, k_all, v_all, ki_all, rel_bias, k_sel)

    out = lax.map(one_block, (blocks(q), blocks(qi), blocks(wi), q_pos))
    out = jnp.swapaxes(out, 0, 1).reshape(B, nb * bq, N_HEADS, HEAD_DIM)
    return out[:, :Q]

def multi_pool(p):
    B, L, C = p.shape
    pf = p.astype(jnp.float32)
    c0 = jnp.concatenate([jnp.zeros((B, 1, C), jnp.float32), jnp.cumsum(pf, axis=1)], axis=1)
    t = jnp.arange(L, dtype=jnp.int32)
    outs = []
    for g, w in enumerate(POOL_WINDOWS):
        sl = slice(g * POOL_GROUP_DIM, (g + 1) * POOL_GROUP_DIM)
        lo = jnp.maximum(t + 1 - w, 0)
        s = c0[:, 1:, sl] - c0[:, lo, sl]
        cnt = (t + 1 - lo).astype(jnp.float32)
        outs.append(s / cnt[None, :, None] - pf[:, :, sl])
    return jnp.concatenate(outs, axis=-1).astype(p.dtype)

def merge_branches(attn, pooled, ga, gb, w_pool_mix, pool_scale, w_br_attn, w_br_pool, w_out):
    lead = attn.shape[:-2]
    a = attn.reshape(*lead, ATTN_WIDTH) @ w_br_attn
    pg = pooled.reshape(*lead, POOL_GROUPS, POOL_GROUP_DIM)
    pm = jnp.einsum('...gc,gcd->...gd', pg, w_pool_mix).reshape(*lead, POOL_WIDTH) * pool_scale
    b = pm @ w_br_pool
    return (jax.nn.sigmoid(ga) * a + jax.nn.sigmoid(gb) * b) @ w_out

def moe_ffn(h, w_router, b_router, w_gu, b_gu, w_down, b_down):
    shp = h.shape
    x = h.reshape(-1, D_MODEL)
    N = x.shape[0]
    logits = (x @ w_router).astype(jnp.float32) + b_router.astype(jnp.float32)
    top_v, top_e = lax.top_k(logits, TOP_EXPERTS)
    gates = jax.nn.softmax(top_v, axis=-1)
    NK = N * TOP_EXPERTS
    flat_e = top_e.reshape(NK)
    flat_g = gates.reshape(NK)
    flat_t = jnp.arange(NK, dtype=jnp.int32) // TOP_EXPERTS
    order = jnp.argsort(flat_e)
    se = flat_e[order]
    counts = jnp.bincount(flat_e, length=N_EXPERTS)
    padded = (counts + MOE_BLOCK - 1) // MOE_BLOCK * MOE_BLOCK
    pend = jnp.cumsum(padded)
    pstart = pend - padded
    start = jnp.cumsum(counts) - counts
    dest = pstart[se] + jnp.arange(NK, dtype=jnp.int32) - start[se]
    n_blocks = -(-(NK + N_EXPERTS * (MOE_BLOCK - 1)) // MOE_BLOCK)
    n_slots = n_blocks * MOE_BLOCK
    slot_tok = jnp.full((n_slots,), N, jnp.int32).at[dest].set(flat_t[order])
    slot_gate = jnp.zeros((n_slots,), jnp.float32).at[dest].set(flat_g[order])
    block_e = jnp.minimum(jnp.searchsorted(pend, jnp.arange(n_blocks, dtype=jnp.int32) * MOE_BLOCK, side='right'), N_EXPERTS - 1)
    x_ext = jnp.concatenate([x, jnp.zeros((1, D_MODEL), x.dtype)], axis=0)
    xb = x_ext[slot_tok].reshape(n_blocks, MOE_BLOCK, D_MODEL)

    def expert_block(args):
        xe, e = args
        gu = xe @ w_gu[e] + b_gu[e]
        gate = jnp.minimum(gu[:, :D_EXPERT], SWIGLU_LIMIT)
        up = jnp.clip(gu[:, D_EXPERT:], -SWIGLU_LIMIT, SWIGLU_LIMIT)
        act = (up + 1.0) * gate * jax.nn.sigmoid(SWIGLU_ALPHA * gate)
        return act @ w_down[e] + b_down[e]

    yb = lax.map(expert_block, (xb, block_e)).reshape(n_slots, D_MODEL)
    y = jnp.zeros((N + 1, D_MODEL), jnp.float32).at[slot_tok].add(yb.astype(jnp.float32) * slot_gate[:, None])[:N]
    return y.astype(h.dtype).reshape(shp)

def paged_rows(pool, table):
    rows = pool[table]
    return rows.reshape(table.shape[0], table.shape[1] * pool.shape[1], *pool.shape[2:])

def setup_inputs(seed: int = 0) -> dict:
    key = jax.random.key(seed)
    ks = jax.random.split(key, 24)
    f32 = jnp.float32
    n_pages = PAST_LEN // PAGE_SIZE
    n_used = DEC_BATCH * n_pages
    n_pool = n_used + n_used // 4

    def nrm(k, shape, scale):
        return jax.random.normal(k, shape, f32) * scale

    return {
        'x_prompt': nrm(ks[0], (BATCH, SEQ, D_MODEL), 1.0),
        'x_sample': nrm(ks[1], (DEC_BATCH, DEC_SEQ, D_MODEL), 1.0),
        'cache_k': nrm(ks[2], (DEPTH, n_pool, PAGE_SIZE, N_HEADS, HEAD_DIM), 1.0),
        'cache_v': nrm(ks[3], (DEPTH, n_pool, PAGE_SIZE, N_HEADS, HEAD_DIM), 1.0),
        'cache_kidx': nrm(ks[4], (DEPTH, n_pool, PAGE_SIZE, IDX_DIM), 1.0),
        'state_pool': nrm(ks[5], (DEPTH, DEC_BATCH, POOL_STATE, POOL_WIDTH), 1.0),
        'page_table': jax.random.permutation(ks[6], n_pool)[:n_used].reshape(DEC_BATCH, n_pages).astype(jnp.int32),
        'meta_tokens': nrm(ks[7], (N_META, D_MODEL), 1.0),
        'rel_bias': nrm(ks[8], (N_BUCKETS, N_HEADS), 0.5),
        'g_mix': 1.0 + nrm(ks[9], (DEPTH, D_MODEL), 0.05),
        'w_in': nrm(ks[10], (DEPTH, D_MODEL, IN_WIDTH), D_MODEL ** -0.5),
        'w_pool_mix': nrm(ks[11], (DEPTH, POOL_GROUPS, POOL_GROUP_DIM, POOL_GROUP_DIM), POOL_GROUP_DIM ** -0.5),
        'pool_scale': 1.0 + nrm(ks[12], (DEPTH, POOL_WIDTH), 0.05),
        'w_br_attn': nrm(ks[13], (DEPTH, ATTN_WIDTH, D_MODEL), ATTN_WIDTH ** -0.5),
        'w_br_pool': nrm(ks[14], (DEPTH, POOL_WIDTH, D_MODEL), POOL_WIDTH ** -0.5),
        'w_out': nrm(ks[15], (DEPTH, D_MODEL, D_MODEL), D_MODEL ** -0.5),
        'g_ffn': 1.0 + nrm(ks[16], (DEPTH, D_MODEL), 0.05),
        'w_router': nrm(ks[17], (DEPTH, D_MODEL, N_EXPERTS), D_MODEL ** -0.5),
        'b_router': nrm(ks[18], (DEPTH, N_EXPERTS), 0.01),
        'w_gate_up': nrm(ks[19], (DEPTH, N_EXPERTS, D_MODEL, 2 * D_EXPERT), D_MODEL ** -0.5),
        'b_gate_up': nrm(ks[20], (DEPTH, N_EXPERTS, 2 * D_EXPERT), 0.01),
        'w_down': nrm(ks[21], (DEPTH, N_EXPERTS, D_EXPERT, D_MODEL), D_EXPERT ** -0.5),
        'b_down': nrm(ks[22], (DEPTH, N_EXPERTS, D_MODEL), 0.01),
        'g_final': 1.0 + nrm(ks[23], (D_MODEL,), 0.05),
    }

def reference(x_prompt, x_sample, cache_k, cache_v, cache_kidx, state_pool, page_table, meta_tokens, rel_bias, g_mix, w_in, w_pool_mix, pool_scale, w_br_attn, w_br_pool, w_out, g_ffn, w_router, b_router, w_gate_up, b_gate_up, w_down, b_down, g_final):
    b_p, s_p, _ = x_prompt.shape
    s_s = x_sample.shape[1]
    n_pages = page_table.shape[1]
    past_len = n_pages * PAGE_SIZE
    k_sel_p = min(TOPK_MAX, s_p // 4)
    k_sel_s = min(TOPK_MAX, (past_len + s_s) // 4)

    meta = jnp.broadcast_to(meta_tokens[None].astype(x_prompt.dtype), (b_p, N_META, D_MODEL))
    xp = jnp.concatenate([meta, x_prompt], axis=1)
    xs = x_sample
    nk_p, nv_p, nki_p, npool_p = [], [], [], []
    nk_s, nv_s, nki_s, npool_s = [], [], [], []

    for l in range(DEPTH):
        h = rms_norm(xp, g_mix[l])
        q, k, v, qi, ki, wi, p, ga, gb = project(h, w_in[l])
        attn = blocked_attention(q, qi, wi, 0, k, v, ki, rel_bias, k_sel_p)
        pooled = multi_pool(p)
        xp = xp + merge_branches(attn, pooled, ga, gb, w_pool_mix[l], pool_scale[l], w_br_attn[l], w_br_pool[l], w_out[l])
        xp = xp + moe_ffn(rms_norm(xp, g_ffn[l]), w_router[l], b_router[l], w_gate_up[l], b_gate_up[l], w_down[l], b_down[l])
        nk_p.append(k)
        nv_p.append(v)
        nki_p.append(ki)
        npool_p.append(p[:, -POOL_STATE:])

        h = rms_norm(xs, g_mix[l])
        q, k, v, qi, ki, wi, p, ga, gb = project(h, w_in[l])
        k_all = jnp.concatenate([paged_rows(cache_k[l], page_table).astype(k.dtype), k], axis=1)
        v_all = jnp.concatenate([paged_rows(cache_v[l], page_table).astype(v.dtype), v], axis=1)
        ki_all = jnp.concatenate([paged_rows(cache_kidx[l], page_table).astype(ki.dtype), ki], axis=1)
        attn = blocked_attention(q, qi, wi, past_len, k_all, v_all, ki_all, rel_bias, k_sel_s)
        p_ext = jnp.concatenate([state_pool[l].astype(p.dtype), p], axis=1)
        pooled = multi_pool(p_ext)[:, POOL_STATE:]
        xs = xs + merge_branches(attn, pooled, ga, gb, w_pool_mix[l], pool_scale[l], w_br_attn[l], w_br_pool[l], w_out[l])
        xs = xs + moe_ffn(rms_norm(xs, g_ffn[l]), w_router[l], b_router[l], w_gate_up[l], b_gate_up[l], w_down[l], b_down[l])
        nk_s.append(k)
        nv_s.append(v)
        nki_s.append(ki)
        npool_s.append(p_ext[:, -POOL_STATE:])

    y_prompt = rms_norm(xp, g_final)[:, N_META:]
    y_sample = rms_norm(xs, g_final)
    return (y_prompt, y_sample, jnp.stack(nk_p), jnp.stack(nv_p), jnp.stack(nki_p), jnp.stack(npool_p), jnp.stack(nk_s), jnp.stack(nv_s), jnp.stack(nki_s), jnp.stack(npool_s))


_drawn_inputs = setup_inputs


def setup_inputs(seed=0):
    import zlib

    import numpy as np

    out = dict(_drawn_inputs(seed))
    spreads = {}
    factors = {'b_gate_up': 8.0, 'b_down': 8.0}
    for name, (base, spread) in spreads.items():
        noise = np.random.default_rng([zlib.crc32(name.encode()), seed]).standard_normal(out[name].shape)
        drawn = base * np.exp(spread * noise) if base else spread * noise
        out[name] = jnp.asarray(drawn.astype(out[name].dtype))
    for name, factor in factors.items():
        out[name] = (out[name] * factor).astype(out[name].dtype)
    return out
```

```python
from contextlib import ExitStack

import concourse.bass as bass
import numpy as np
from concourse import mybir

F32 = mybir.dt.float32
I32 = mybir.dt.int32
U32 = mybir.dt.uint32
ALU = mybir.AluOpType
ACT = mybir.ActivationFunctionType
AX = mybir.AxisListType
SP = mybir.EngineType.SP

P = 128
D = 1024
KD = D // P
META, SEQ, NS = 16, 512, 8
NP_ = META + SEQ
NT = NP_ + NS
HALF = NT // 2
NTILE = 5
TAIL = NT - 4 * P
H, HD = 8, 64
AW = H * HD
PAGE, NPAGE, NPOOL = 128, 8, 80
PAST = PAGE * NPAGE
KEYS_S = PAST + 1
TOPK_P = min(256, SEQ // 4)
TOPK_S = min(256, KEYS_S // 4)
NB = 32
PG = 4
NE, TOPE = 32, 4
CAP = 96
PASSES = -(-NT // CAP)
SELS = NE + 1
CHUNKS = 4
STRIP = 640
OUT = -1.0e30
NONCAUSAL = -3.0e38
TAKEN = -3.3e38
EPS = 1e-6
PAD = 16

RING = 4096
KEYS = [min(P * (t + 1), NP_) for t in range(NTILE)]
ROWS = [P, P, P, P, META]
TROWS = [P, P, P, P, TAIL]
SCORE_AT = {1: 0, 2: 256, 3: 640, 4: 1152}
SCORE_W = 1680

C_ID, C_TRI, C_IOTA, C_EXP, C_TOK, C_TRASH, C_RCNT, C_OFFD, C_WSEL, C_VALID, C_W = 0, 128, 256, 352, 384, 389, 390, 454, 462, 470, 471


def build_step(nc, xT, xnat, consts, g_mix, w_mt, w_wi, w_v, w_mix, pool_scale, w_bra, w_brp, w_out,
               w_router, b_router, b_gu, w_gu, w_down, b_down, g_ffn, g_final, bias_strip, bias_s,
               cache_kT, cache_v, cache_kiT, page_table, state, stateT,
               o_y, o_kT, o_v, o_kiT, o_pT, o_state):
    ctx = ExitStack()
    with ctx:
        def sb(name, shape, dt=F32):
            return ctx.enter_context(nc.sbuf_tensor(name, shape, dt))

        def sem(name):
            return ctx.enter_context(nc.semaphore(name))

        def dram(name, shape, dt=F32):
            return nc.dram_tensor(name, shape, dt).ap()

        y_acc = dram("y_acc", (NT + CAP, D))
        h_rows = dram("h_rows", (NT + CAP, D))
        wi_row = dram("wi_row", (NS, H))

        W6 = sb("weight_ring", [P, 6 * RING])
        X1 = sb("region_x1", [P, KD * NT])
        X2 = sb("region_x2", [P, KD * NT])
        HR = sb("region_h", [P, KD * NT])
        QK = sb("region_qk", [P, 8 * NT])
        QI = sb("region_qi", [P, 4 * NT])
        KI = sb("region_ki", [P, NT])
        VN = sb("region_v", [P, NTILE * AW])
        WR = sb("region_w", [P, 4 * 1024])
        cst = sb("cst", [P, C_W])
        ones = sb("ones", [P, P])
        zq = sb("zq", [P, 264])
        lg_s = sb("lg_s", [P, 9, 64])
        maskT = sb("maskT", [P, 9, NS])
        wr_sb = sb("wr_sb", [P, KD, NE])
        smalls = sb("smalls", [P, 212])

        def part(region, at, *shape):
            n = int(np.prod(shape))
            v = region[:, at:at + n]
            names = "abcd"[:len(shape)]
            if len(shape) == 1:
                return v
            return v.rearrange(f"p ({' '.join(names)}) -> p {' '.join(names)}", **dict(zip(names[1:], shape[1:])))

        def slot(n):
            return n * RING

        ident = cst[:, C_ID:C_ID + P]
        tri = cst[:, C_TRI:C_TRI + P]
        iota96 = cst[:, C_IOTA:C_IOTA + CAP]
        iota_e = cst[:, C_EXP:C_EXP + NE]
        tokid = cst[:, C_TOK:C_TOK + NTILE]
        trash = cst[:, C_TRASH:C_TRASH + 1]
        rcnt = cst[:, C_RCNT:C_RCNT + 64].rearrange("p (g t) -> p g t", g=PG)
        offd = cst[0:NS, C_OFFD:C_OFFD + NS]
        wsel = cst[0:64, C_WSEL:C_WSEL + NS]
        valid = cst[:, C_VALID:C_VALID + 1]

        x_in = part(X1, 0, KD, NT)
        sq = part(X2, 0, KD, NT)
        hT = part(HR, 0, KD, NT)
        qT = part(QK, 0, 4, NT)
        kT = part(QK, 4 * NT, 4, NT)
        qiT = part(QI, 0, 4, NT)
        attnT = part(QI, 0, 4, NT)
        kiT = KI[:, :]
        vN = part(VN, 0, NTILE, AW)
        wring = part(WR, 0, 4, 1024)
        w_v_sb = part(W6, slot(5), KD, AW)
        kv = [part(W6, slot(n), NPAGE, AW) for n in range(2)]
        pT = part(W6, slot(2), PG, PAD + NT)
        pool_a = part(W6, slot(2) + 2208, PAD + NT)
        pool_b = part(W6, slot(2) + 2760, PAD + NT)
        mix_sb = part(W6, slot(2) + 3312, PG, P)
        wi_sb = part(W6, slot(2) + 3824, KD, H)
        o_sb = part(W6, slot(2), 512)
        strip = part(W6, slot(3), H, STRIP)
        score = part(W6, slot(3) + H * STRIP, SCORE_W)
        score_s = part(W6, slot(3) + H * STRIP + SCORE_W, KEYS_S)
        zi = part(W6, slot(3) + H * STRIP + SCORE_W + 1032, 320)
        lg = [part(W6, slot(5) + 528 * n, 528) for n in range(3)]
        mb = [part(W6, slot(5) + 1584 + 528 * n, 528) for n in range(2)]
        pt = [part(W6, slot(5) + 2640 + 512 * n, 512) for n in range(2)]
        causal0 = part(W6, slot(5) + 3664, P)
        kidx = part(X1, 0, 4, KEYS_S)
        relu_p = [part(X2, 528 * n, 528) for n in range(2)]
        relu_s = part(X2, 1056, KEYS_S)
        stT = part(X2, 2112, PG * NS, 15)
        sga = part(X1, 0, KD, NT)
        sbb = part(X2, 0, KD, NT)
        btmp = KI[:, :]
        wo = [part(HR, 0, KD, 512), part(W6, slot(5), KD, 512)]

        def xn(t):
            return part(QK, D * t, D) if t < 4 else part(VN, 0, D)

        def hf(t):
            return part(X2, D * t, D) if t < 4 else part(VN, D, D)
        zrow = part(VN, 2 * D, 512)
        hfT = [part(QI, n * 1024, KD, P) for n in range(2)]
        gffn = part(WR, 0, D)
        gfin = part(WR, D, D)
        rt_log = part(WR, 2048, NTILE, NE)
        rt_eq = part(WR, 2208, NTILE, TOPE, NE)
        rt_eg = part(WR, 2848, NTILE, TOPE, NE)
        rt_m = part(WR, 3488, NTILE, NE)
        rt_g = part(WR, 3648, NTILE, NE)
        rt_e = part(WR, 3808, NTILE, 8)
        rt_w = part(WR, 3848, NTILE, TOPE)
        rt_br = part(WR, 3872, NE)
        rt_cnt = part(WR, 3904, NE)
        b_gu_sb = part(KI, 0, NE, 16)
        posv = part(X2, 0, NTILE, SELS)
        gx = part(X2, 165, NTILE, SELS, 3)
        gT = part(X2, 700, NTILE, P)
        bd_sb = part(X2, 1340, D)
        xg = [part(HR, D * n, D) for n in range(2)]
        ysc = [part(HR, D * (2 + n), D) for n in range(2)]
        cmpm = [part(X1, NTILE * CAP * n, NTILE, CAP) for n in range(2)]
        hTe = part(X1, 960, KD, CAP)
        actT = part(X1, 1728, KD, CAP)
        gu_t = [part(X1, 2496 + 384 * n, 4, CAP) for n in range(2)]
        sg_t = [part(X1, 3264 + 192 * n, 2, CAP) for n in range(2)]
        gs_t = part(X1, 3648, 2, CAP)
        yf = part(W6, 0, NTILE, D)
        junk = part(W6, slot(2), D)

        def small(at, n=1):
            return smalls[:, at:at + n]
        gmix_sb = small(0, 8)
        psc_sb = small(8, 4)
        wi_nat = small(12, 40).rearrange("p (t h) -> p t h", h=H)
        wcol = small(52)
        wblk = small(53, 8)
        max8 = small(61, 8)
        nmax = small(69, 40)
        esum = small(109, 40)
        rsum = small(149, 40)
        rms = small(189, 5)
        rms2 = small(194, 5)
        m64 = small(199)
        eps_t = small(200)
        sum4 = small(201, 5)
        gcol = [small(206 + n) for n in range(2)]
        spare = small(208)
        unused = [small(209 + n) for n in range(2)]
        iota_b = part(X1, 3840, CAP)
        top_v = part(WR, 3936, NTILE, 8)
        top_i = part(WR, 3976, NTILE, 8).bitcast(U32)
        bias_sb = sb("bias_sb", [P, 9, H])
        dg = part(W6, slot(2) + 3888, 64)[0:64]
        m_all = part(W6, slot(2) + 3952, 64)
        rs_s = part(W6, slot(2) + 4016, 64)
        v_new = part(W6, slot(2) + 2208, AW)[0:NS]
        idx_i = [sb(f"idx_i{n}", [P, 1], I32) for n in range(2)]
        cnt_i = sb("cnt_i", [1, 8], I32)
        pt_sb = sb("pt_sb", [1, NS * NPAGE], I32)

        PS = ctx.enter_context(nc.psum_tensor("PS", [P, 8, 512], F32))
        PSF = PS[:, :, :].rearrange("p a b -> p (a b)")

        def bank(n, w=512, at=0):
            return PSF[:, 512 * n + at:512 * n + at + w]
        PB = [PS[:, 0:2, :], PS[:, 2:4, :]]
        AB = [PSF[:, 4 * 512:6 * 512], PSF[:, 6 * 512:8 * 512]]
        SB_ = [PSF[:, 6 * 512:8 * 512], PSF[:, 0:1024]]
        PTB = [bank(2), bank(3)]
        L_s = bank(4).rearrange("p (t x) -> p t x", t=8)
        L_n = bank(5, 64)
        PO = bank(5, 264)
        O_p = bank(4)

        names = """pool_may kinew_set Lqk_done acc_done acc_init act_ready act_taken all_added attn_s_done b_mult bd_in bgu_in
        causal_done clamp_done cmp_ready cnt_ready cst_in dn_half dn_ready dots_ready dve_step
        dve_taken eps_set exp_done exps_done fin_gb fin_rs fin_sq fin_y gT_done gated gb_ready gmix_in
        gtr_ready gu_ready gu_taken hTe_ready h_done hfT_ready hfT_taken hf_done idx_ready kidx_in kvu
        late_in lgp_done lgs_done m_done m_ready mask_done mb_done mb_ready mdiag_done mxT_ready
        oT_ready oT_taken o_norm ones_set out_done po_step pool_done pool_pad proj_done pt_ready
        pt_taken pv_head rank_ready relu_done router_ready row_ms s_ready sel_ready sidx_taken sig_done
        slot_ready slots_moved smT_ready small_in smask_done sq_done stT_in strip_in sums_ready
        unused_done up_done vnew_in wblk_done wcol_in wi_out wo0_in wo1_in wv_in x_in xn_in xt_ready
        y_ready yf_in zero_rows zero_set zi_set zq_done ztmp_in""".split()
        S = {n: sem(n) for n in names}
        w_full = [sem(f"w_full{n}") for n in range(4)]
        kv_full = [sem(f"kv_full{n}") for n in range(2)]
        r_full = [sem(f"ring_full{n}") for n in range(6)]
        gath = [sem(f"gathered{n}") for n in range(2)]
        scat = [sem(f"scattered{n}") for n in range(2)]

        J_SS, J_QI, J_KI, J_WI, J_K, J_Q, J_P, J_V, J_MIX, J_GATE = 0, 1, 5, 6, 7, 11, 15, 19, 24, 28
        J_A, J_WO, J_TR = 52, 60, 65
        N_MT = 17
        ITEMS = N_MT + 3 * KD + KD

        def job_of(n):
            if n < 5:
                return J_QI + n
            if n < N_MT:
                return J_K + n - 5
            return J_GATE + n - N_MT if n < N_MT + 3 * KD else J_A + n - N_MT - 3 * KD
        DOTS = [(t, h) for t in (4, 3, 2, 1) for h in range(H)]
        HEADS = [(t, h) for t in range(NTILE) for h in range(H)]

        def link(eng, ins, name, count):
            count[0] += 1
            ins.then_inc(S[name], 1)
            eng.wait_ge(S[name], count[0])

        block = ctx.enter_context(nc.Block())

        @block.sync
        def _(sp):
            def item(n):
                if n >= 4:
                    sp.wait_ge(S["proj_done"], job_of(n - 4) + 1)
                if n < N_MT:
                    src, w = w_mt[n], 1024
                elif n < N_MT + 3 * KD:
                    d, k = divmod(n - N_MT, 3)
                    src, w = ((w_mt[N_MT + 2 * d], 1024), (w_brp[d], 512), (w_mt[N_MT + 2 * d + 1], 1024))[k]
                else:
                    src, w = w_bra[n - N_MT - 3 * KD], 512
                sp.dma_start(wring[:, n % 4, 0:w], src).then_inc(w_full[n % 4], 16)

            def pages(n):
                if n >= 2:
                    sp.wait_ge(S["kvu"], n - 1)
                cache = cache_kT if n < NS else cache_v
                b = n % NS
                _, found = nc.values_load_multi_w_load_instructions(pt_sb[0:1, NPAGE * b:NPAGE * b + NPAGE], [SP], min_val=0, max_val=NPOOL - 1)
                for j, page in enumerate(found):
                    sp.dma_start(kv[n % 2][:, j, :], cache[bass.ds(page, 1)].rearrange("a p x -> (a p) x")).then_inc(kv_full[n % 2], 16)

            sp.dma_start(x_in, xT).then_inc(S["x_in"], 16)
            sp.dma_start(cst[:, :], consts).then_inc(S["cst_in"], 16)
            sp.dma_start(gmix_sb, g_mix).then_inc(S["gmix_in"], 16)
            sp.dma_start(pt_sb[:, :], page_table).then_inc(S["small_in"], 16)
            sp.dma_start(psc_sb, pool_scale).then_inc(S["small_in"], 16)
            sp.dma_start(wi_sb, w_wi).then_inc(S["small_in"], 16)
            sp.dma_start(mix_sb, w_mix).then_inc(S["small_in"], 16)
            sp.dma_start(wr_sb[:, :, :], w_router).then_inc(S["small_in"], 16)
            sp.dma_start(bias_sb[:, :, :], bias_s).then_inc(S["small_in"], 16)
            for n in range(4):
                item(n)
            sp.wait_ge(S["small_in"], 96)
            sp.wait_ge(S["h_done"], KD)
            for b in range(NS):
                _, found = nc.values_load_multi_w_load_instructions(pt_sb[0:1, NPAGE * b:NPAGE * b + NPAGE], [SP], min_val=0, max_val=NPOOL - 1)
                for g, page in enumerate(found):
                    lo = 64 * (b % 2)
                    sp.dma_start(kidx[lo:lo + 64, b // 2, g * PAGE:g * PAGE + PAGE], cache_kiT[bass.ds(page, 1)].rearrange("a p x -> (a p) x"))\
                        .then_inc(S["kidx_in"], 16)
            sp.dma_start(stT, stateT).then_inc(S["stT_in"], 16)
            sp.dma_start(w_v_sb, w_v).then_inc(S["wv_in"], 16)
            for n in range(4, 9):
                item(n)
            sp.dma_start(strip, bias_strip).then_inc(S["strip_in"], 16)
            sp.dma_start(o_state, state[:, 1:, :]).then_inc(S["out_done"], 16)
            for n in range(9, 12):
                item(n)
            pages(0)
            pages(1)
            for n in range(12, N_MT + 4):
                item(n)
            for n in range(2, NS + 1):
                pages(n)
            sp.wait_ge(S["act_taken"], J_V + NTILE)
            sp.dma_start(o_kT, kT).then_inc(S["out_done"], 16)
            sp.dma_start(o_kiT, kiT[0:64, :]).then_inc(S["out_done"], 16)
            sp.wait_ge(S["pool_done"], PG)
            sp.dma_start(v_new[:, :], vN[META:META + NS, 4, :]).then_inc(S["vnew_in"], 16)
            sp.dma_start(o_v[0:4 * P].rearrange("(t p) x -> p t x", p=P), vN[:, 0:4, :]).then_inc(S["out_done"], 16)
            sp.dma_start(o_v[4 * P:NT], vN[0:TAIL, 4, :]).then_inc(S["out_done"], 16)
            for d in range(KD):
                for k in range(3):
                    item(N_MT + 4 + 3 * d + k)
                if NS + 1 + d < 2 * NS:
                    pages(NS + 1 + d)
            sp.wait_ge(S["act_taken"], J_A)
            sp.dma_start(wo[0], w_out[0]).then_inc(S["wo0_in"], 16)

            def ring_load(c, e):
                if c < CHUNKS:
                    src = w_gu[bass.ds(e, 1), c].rearrange("a p x -> (a p) x")
                else:
                    src = w_down[bass.ds(e, 1), c - CHUNKS].rearrange("a p x -> (a p) x")
                sp.dma_start(W6[:, slot(c):slot(c + 1)], src).then_inc(r_full[c], 16)

            sp.wait_ge(S["kvu"], 2 * NS)
            for c in range(2):
                ring_load(c, 0)
            sp.wait_ge(S["oT_taken"], NTILE)
            sp.dma_start(wo[1], w_out[1]).then_inc(S["wo1_in"], 16)
            for t in range(NTILE):
                sp.dma_start(xn(t)[0:TROWS[t]], xnat[t * P:t * P + TROWS[t]]).then_inc(S["xn_in"], 16)
            for n in range(N_MT + 4 + 3 * KD, ITEMS):
                item(n)
            for c in range(2, 5):
                ring_load(c, 0)
            sp.dma_start(b_gu_sb, b_gu).then_inc(S["bgu_in"], 16)
            sp.wait_ge(S["proj_done"], J_A + KD)
            sp.dma_start(gffn, g_ffn.partition_broadcast(P)).then_inc(S["late_in"], 16)
            sp.dma_start(gfin, g_final.partition_broadcast(P)).then_inc(S["late_in"], 16)
            sp.dma_start(rt_br, b_router.partition_broadcast(P)).then_inc(S["late_in"], 16)
            for t in range(NTILE):
                sp.wait_ge(S["dve_taken"], KD + t + 1)
                sp.dma_start(y_acc[t * P:t * P + TROWS[t]], xn(t)[0:TROWS[t]]).then_inc(S["acc_init"], 16)
                sp.wait_ge(S["hf_done"], t + 1)
                sp.dma_start(h_rows[t * P:t * P + TROWS[t]], hf(t)[0:TROWS[t]]).then_inc(S["acc_init"], 16)
            sp.wait_ge(S["dve_taken"], KD + NTILE)
            ring_load(5, 0)
            sp.wait_ge(S["acc_init"], 16 * 2 * NTILE)
            sp.wait_ge(S["hfT_ready"], NTILE)
            sp.dma_start(bd_sb[0:NE], b_down).then_inc(S["bd_in"], 16)

            def experts(b, first):
                with sp.Fori(first, NE) as e:
                    for c in range(CHUNKS):
                        sp.wait_ge(S["gu_ready"], (b * NE + e - 1) * CHUNKS + c + 1)
                        ring_load(c, e)
                    for c, half in enumerate(("dn_half", "dn_ready")):
                        sp.wait_ge(S[half], b * NE + e)
                        ring_load(CHUNKS + c, e)
            experts(0, 1)
            sp.wait_ge(S["cnt_ready"], 1)
            most = sp.value_load(cnt_i[0:1, 0:1], min_val=0, max_val=NT)
            with sp.Fori(1, PASSES) as b:
                with sp.If(b * CAP < most):
                    experts(b, 0)
            sp.wait_ge(S["all_added"], 1)
            sp.dma_start(yf[:, 0:4, :], y_acc[0:4 * P].rearrange("(t p) x -> p t x", p=P)).then_inc(S["yf_in"], 16)
            sp.dma_start(yf[0:TAIL, 4, :], y_acc[4 * P:NT]).then_inc(S["yf_in"], 16)
            for t in range(NTILE):
                sp.wait_ge(S["fin_y"], t + 1)
                sp.dma_start(o_y[t * P:t * P + TROWS[t]], yf[0:TROWS[t], t, :]).then_inc(S["out_done"], 16)
            sp.wait_ge(S["out_done"], 16 * (5 + NTILE))

        @block.gpsimd
        def _(po):
            n = [0]
            po.wait_ge(S["cst_in"], 16)
            po.memset(ones[:, :], 1.0).then_inc(S["ones_set"], 1)
            po.memset(eps_t, EPS).then_inc(S["eps_set"], 1)
            po.memset(pT[:, :, 0:PAD], 0.0)
            po.memset(pool_a[:, 0:PAD], 0.0)
            po.memset(pool_b[:, 0:PAD], 0.0).then_inc(S["pool_pad"], 1)
            po.memset(zi, 0.0)
            po.memset(zq[:, :], 0.0).then_inc(S["zero_set"], 1)
            po.memset(lg_s[:, 8, :], OUT).then_inc(S["zero_set"], 1)
            po.wait_ge(S["act_taken"], J_QI + 4)
            po.wait_ge(S["zero_set"], 2)
            ziv = zi.rearrange("p (j x) -> p j x", x=80)
            for r in range(2):
                for hp in range(2):
                    for j in range(4):
                        po.dma_start(ziv[64 * r:64 * r + 64, j, 8 * r + hp:8 * r + hp + 8:2],
                                     qiT[64 * hp:64 * hp + 64, :, NP_ + r + 2 * j], allow_slow_non_contiguous=True).then_inc(S["zi_set"], 16)
            po.wait_ge(S["act_taken"], J_KI + 1)
            po.wait_ge(S["h_done"], KD)
            for r in range(2):
                po.tensor_copy(kidx[64 * r:64 * r + 64, :, PAST], kiT[64 * r:64 * r + 64, NP_ + r:NT:2]).then_inc(S["kinew_set"], 1)
            po.wait_ge(S["kinew_set"], 2)
            po.wait_ge(S["act_taken"], J_WI + 1)
            po.dma_start(wi_row, wi_nat[META:META + NS, 4, :]).then_inc(S["wi_out"], 16)
            po.wait_ge(S["wi_out"], 16)
            po.dma_start(wcol[0:64], wi_row.rearrange("b (h o) -> (b h) o", o=1)).then_inc(S["wcol_in"], 16)
            po.wait_ge(S["wcol_in"], 16)
            po.tensor_scalar(wblk[0:64], wsel, wcol[0:64], None, ALU.mult).then_inc(S["wblk_done"], 1)
            po.wait_ge(S["wblk_done"], 1)
            for i, t in enumerate((4, 3, 2, 1)):
                po.wait_ge(S["acc_done"], H * (i + 1))
                v = score[0:ROWS[t], SCORE_AT[t] + P * t:SCORE_AT[t] + KEYS[t]]
                po.affine_select(out=v, in_=v, compare_op=ALU.is_ge, fill=NONCAUSAL, base=0,
                                 pattern=[[-1, ROWS[t]]], channel_multiplier=1).then_inc(S["causal_done"], 1)
                po.wait_ge(S["causal_done"], i + 1)
            po.wait_ge(S["pool_pad"], 1)
            po.wait_ge(S["stT_in"], 16)
            for g in range(PG):
                w = 2 << g
                po.wait_ge(S["act_taken"], J_P + g + 1)
                src = pT[:, g, :]
                for s in range(g + 1):
                    dst = pool_a if s % 2 == 0 else pool_b
                    link(po, po.tensor_tensor(dst[:, PAD:PAD + NP_], src[:, PAD:PAD + NP_],
                                              src[:, PAD - (1 << s):PAD + NP_ - (1 << s)], ALU.add), "po_step", n)
                    src = dst
                sd = src[:, PAD + NP_:PAD + NT]
                st = stT[:, NS * g:NS * g + NS, :]
                link(po, po.tensor_tensor(sd, pT[:, g, PAD + NP_:PAD + NT], st[:, :, 14], ALU.add), "po_step", n)
                for k in range(2, w):
                    link(po, po.tensor_tensor(sd, sd, st[:, :, 15 - k], ALU.add), "po_step", n)
                link(po, po.tensor_tensor(src[:, PAD:2 * PAD], src[:, PAD:2 * PAD], rcnt[:, g, :], ALU.mult), "po_step", n)
                link(po, po.tensor_scalar(src[:, 2 * PAD:], src[:, 2 * PAD:], 1.0 / w, None, ALU.mult), "po_step", n)
                po.dma_start(o_pT[:, g, :], pT[:, g, PAD + NP_ - 15:PAD + NT]).then_inc(S["ztmp_in"], 16)
                po.wait_ge(S["ztmp_in"], 16 * (g + 1))
                po.tensor_tensor(pT[:, g, PAD:], src[:, PAD:], pT[:, g, PAD:], ALU.subtract).then_inc(S["pool_done"], 1)
                po.wait_ge(S["pool_done"], g + 1)
            for d in range(KD):
                po.wait_ge(S["act_taken"], J_GATE + 3 * d + 2)
                po.tensor_tensor(sbb[:, d, :], sbb[:, d, :], btmp, ALU.mult).then_inc(S["b_mult"], 1)
                po.wait_ge(S["b_mult"], d + 1)
            po.wait_ge(S["wv_in"], 16)
            po.wait_ge(S["act_taken"], J_V + NTILE)
            link(po, po.memset(causal0, 0.0), "po_step", n)
            link(po, po.affine_select(out=causal0, in_=causal0, compare_op=ALU.is_ge, fill=OUT, base=0,
                                      pattern=[[-1, P]], channel_multiplier=1), "po_step", n)
            po.wait_ge(S["strip_in"], 16)
            for i, (t, h) in enumerate(HEADS):
                if h == 0 and t:
                    po.wait_ge(S["mask_done"], t)
                if i >= 2:
                    po.wait_ge(S["lgp_done"], i - 1)
                r, w = ROWS[t], KEYS[t]
                m = causal0 if t == 0 else score[:, SCORE_AT[t]:SCORE_AT[t] + w]
                po.tensor_tensor(mb[i % 2][0:r, 0:w], m[0:r], strip[0:r, h, 512 - P * t:512 - P * t + w], ALU.add)\
                    .then_inc(S["mb_done"], 1)
                po.wait_ge(S["mb_done"], i + 1)
            po.wait_ge(S["m_done"], KD)
            link(po, po.memset(zrow[0:CAP], 0.0), "po_step", n)
            for a in range(2):
                po.dma_start(y_acc[NT:NT + CAP, 512 * a:512 * a + 512], zrow[0:CAP]).then_inc(S["zero_rows"], 16)
                po.dma_start(h_rows[NT:NT + CAP, 512 * a:512 * a + 512], zrow[0:CAP]).then_inc(S["zero_rows"], 16)
            po.wait_ge(S["zero_rows"], 64)
            po.wait_ge(S["acc_init"], 16 * 2 * NTILE)

            def gather(b, e, u):
                po.wait_ge(S["idx_ready"], b * SELS + e + 1)
                po.sem_inc(S["pool_may"], 1)
                po.indirect_dma_start(xg[u][0:CAP], None, h_rows, bass.IndirectOffsetOnAxis(ap=idx_i[u][0:CAP, :], axis=0))\
                    .then_inc(gath[u], 16)

            def experts(b):
                gather(b, 0, 0)
                with po.Fori(0, NE // 2) as i:
                    for u in range(2):
                        e = i * 2 + u
                        gather(b, e + 1, 1 - u)
                        if u == 0:
                            po.wait_ge(scat[1], (b * (NE // 2) + i) * 16)
                        else:
                            po.wait_ge(scat[0], (b * (NE // 2) + i + 1) * 16)
                        po.wait_ge(S["y_ready"], b * NE + e + 1)
                        po.sem_inc(S["pool_may"], 1)
                        po.indirect_dma_start(y_acc, bass.IndirectOffsetOnAxis(ap=idx_i[u][0:CAP, :], axis=0),
                                              ysc[u][0:CAP], None, compute_op=ALU.add).then_inc(scat[u], 16)
                po.wait_ge(scat[1], (b * (NE // 2) + NE // 2) * 16)

            po.wait_ge(S["cnt_ready"], 1)
            most = po.value_load(cnt_i[0:1, 0:1], min_val=0, max_val=NT)
            experts(0)
            with po.Fori(1, PASSES) as b:
                with po.If(b * CAP < most):
                    experts(b)
            po.wait_ge(S["cnt_ready"], 1)
            po.memset(spare, 0.0).then_inc(S["all_added"], 1)

        @block.scalar
        def _(act):
            def take(j, dst, src, func=ACT.Copy, scale=1.0):
                act.wait_ge(S["proj_done"], j + 1)
                return nc.scalar.activation(dst, src, func, scale=scale)

            def wide(j):
                return PB[j % 2][:, :, 0:HALF]

            def halves(ap):
                return ap.rearrange("p (a b) -> p a b", a=2)

            act.wait_ge(S["x_in"], 16)
            for k in range(KD):
                act.activation(sq[:, k, :], x_in[:, k, :], ACT.Square).then_inc(S["sq_done"], 1)
            act.wait_ge(S["eps_set"], 1)
            act.wait_ge(S["proj_done"], 1)
            nc.scalar.activation(halves(KI[:, :]), wide(0), ACT.Sqrt, bias=eps_t, scale=1.0 / D).then_inc(S["act_taken"], 1)
            for c in range(4):
                take(J_QI + c, halves(qiT[:, c, :]), wide(J_QI + c)).then_inc(S["act_taken"], 1)
            act.wait_ge(S["h_done"], KD)
            take(J_KI, halves(kiT), wide(J_KI)).then_inc(S["act_taken"], 1)
            act.wait_ge(S["proj_done"], J_WI + 1)
            nc.scalar.activation(wi_nat[:, 0:4, :], PB[J_WI % 2][:, 0, 0:32].rearrange("p (t h) -> p t h", h=H), ACT.Copy)
            nc.scalar.activation(wi_nat[0:TAIL, 4, :], PB[J_WI % 2][0:TAIL, 0, 32:40], ACT.Copy).then_inc(S["act_taken"], 1)
            for i, (t, h) in enumerate(DOTS):
                act.wait_ge(S["dots_ready"], i + 1)
                if i >= 2:
                    act.wait_ge(S["acc_done"], i - 1)
                act.activation(relu_p[i % 2][0:ROWS[t], 0:KEYS[t]], AB[i % 2][0:ROWS[t], 0:KEYS[t]], ACT.Relu)\
                    .then_inc(S["relu_done"], 1)
            act.wait_ge(S["dots_ready"], len(DOTS) + 1)
            act.activation(relu_s[0:64], PSF[0:64, 4 * 512:4 * 512 + KEYS_S], ACT.Relu).then_inc(S["relu_done"], 1)
            for c in range(4):
                take(J_K + c, halves(kT[:, c, :]), wide(J_K + c)).then_inc(S["act_taken"], 1)
            for c in range(4):
                take(J_Q + c, halves(qT[:, c, :]), wide(J_Q + c), scale=HD ** -0.5).then_inc(S["act_taken"], 1)
            act.wait_ge(S["act_taken"], J_Q + 4)
            act.wait_ge(S["zero_set"], 1)
            zqv = zq[:, :].rearrange("p (c x) -> p c x", x=66)
            for hp in range(2):
                act.activation(zqv[64 * hp:64 * hp + 64, :, hp:hp + 64:8], qT[64 * hp:64 * hp + 64, :, NP_:NT], ACT.Copy)\
                    .then_inc(S["zq_done"], 1)
            act.wait_ge(S["pool_pad"], 1)
            for g in range(PG):
                take(J_P + g, halves(pT[:, g, PAD:]), wide(J_P + g)).then_inc(S["act_taken"], 1)
            for t in range(NTILE):
                r = TROWS[t]
                take(J_V + t, vN[0:r, t, :], PB[(J_V + t) % 2][0:r, 0, :]).then_inc(S["act_taken"], 1)
            for g in range(PG):
                act.wait_ge(S["small_in"], 96)
                take(J_MIX + g, halves(pT[:, g, PAD:]), wide(J_MIX + g), scale=psc_sb[:, g:g + 1]).then_inc(S["act_taken"], 1)
            act.wait_ge(S["acc_done"], len(DOTS))
            act.wait_ge(S["sidx_taken"], 1)
            act.wait_ge(S["pool_done"], PG)
            for d in range(KD):
                j = J_GATE + 3 * d
                take(j, halves(sbb[:, d, :]), wide(j), ACT.Sigmoid).then_inc(S["act_taken"], 1)
                if d == 0:
                    act.wait_ge(S["out_done"], 16 * 5)
                else:
                    act.wait_ge(S["b_mult"], d)
                act.wait_ge(S["proj_done"], j + 2)
                nc.scalar.activation(halves(btmp), wide(j + 1), ACT.Copy).then_inc(S["act_taken"], 1)
                take(j + 2, halves(sga[:, d, :]), wide(j + 2), ACT.Sigmoid).then_inc(S["act_taken"], 1)
                if d == 0:
                    act.wait_ge(S["mdiag_done"], 2)
                    act.activation(lg_s[:, :, :], lg_s[:, :, :], ACT.Exp).then_inc(S["exps_done"], 1)

            def pt_out(i):
                t = HEADS[i][0]
                act.wait_ge(S["pt_ready"], i + 1)
                if i >= 2:
                    act.wait_ge(S["pv_head"], i - 1)
                r, nk = ROWS[t], -(-KEYS[t] // P)
                if t < 4:
                    act.activation(pt[i % 2][:, 0:nk * r], PTB[i % 2][:, 0:nk * r], ACT.Copy).then_inc(S["pt_taken"], 1)
                else:
                    act.activation(pt[i % 2][:, 0:4 * r], PTB[i % 2][:, 0:4 * r], ACT.Copy)
                    act.activation(pt[i % 2][0:META, 4 * r:5 * r], PTB[i % 2][0:META, 4 * r:5 * r], ACT.Copy).then_inc(S["pt_taken"], 1)

            def oT_out(t):
                act.wait_ge(S["oT_ready"], t + 1)
                r = ROWS[t]
                act.activation(attnT[:, :, P * t:P * t + r], bank(5, 4 * r).rearrange("p (c r) -> p c r", c=4), ACT.Copy)\
                    .then_inc(S["oT_taken"], 1)

            for i, (t, h) in enumerate(HEADS):
                r, w = ROWS[t], KEYS[t]
                act.wait_ge(S["lgp_done"], i + 1)
                act.activation(lg[i % 3][0:r, 0:w], lg[i % 3][0:r, 0:w], ACT.Exp, bias=nmax[0:r, i:i + 1], scale=-1.0,
                               accum_out=esum[0:r, i:i + 1]).then_inc(S["exp_done"], 1)
                if i:
                    pt_out(i - 1)
                if h == 2 and t:
                    oT_out(t - 1)
            pt_out(len(HEADS) - 1)
            oT_out(NTILE - 1)

            def hfT_out(t):
                j, r = J_TR + t, TROWS[t]
                act.wait_ge(S["hfT_ready"], t + 1)
                if t >= 2:
                    act.wait_ge(S["router_ready"], t - 1)
                act.activation(hfT[t % 2][:, :, 0:r], PSF[:, 1024 * (j % 2):1024 * (j % 2) + KD * r].rearrange("p (k r) -> p k r", k=KD),
                               ACT.Copy).then_inc(S["hfT_taken"], 1)
            for t in range(NTILE):
                r = TROWS[t]
                act.wait_ge(S["dve_taken"], KD + t + 1)
                act.wait_ge(S["m_done"], KD)
                act.activation(hf(t)[0:r], xn(t)[0:r], ACT.Square, accum_out=rms[0:r, t:t + 1]).then_inc(S["row_ms"], 1)
                act.wait_ge(S["row_ms"], 2 * t + 1)
                act.activation(rms[0:r, t:t + 1], rms[0:r, t:t + 1], ACT.Sqrt, bias=eps_t[0:r], scale=1.0 / D).then_inc(S["row_ms"], 1)
                if t:
                    hfT_out(t - 1)
            hfT_out(NTILE - 1)

            act.wait_ge(S["sel_ready"], 1)
            act.activation(rt_w, rt_w, ACT.Exp).then_inc(S["sel_ready"], 1)

            def hTe_out(n):
                act.wait_ge(S["xt_ready"], n)
                act.activation(hTe.rearrange("p (a k) s -> p a (k s)", a=2), PS[:, 2:4, 0:4 * CAP], ACT.Copy).then_inc(S["hTe_ready"], 1)

            def experts(b):
                hTe_out(b * SELS + 1)
                with act.Fori(0, NE // 2) as i:
                    for u in range(2):
                        e = i * 2 + u
                        for c in range(CHUNKS):
                            act.wait_ge(S["clamp_done"], (b * NE + e) * CHUNKS + c + 1)
                            act.activation(sg_t[c % 2], gu_t[c % 2][:, 0:2, :], ACT.Sigmoid, scale=1.702).then_inc(S["sig_done"], 1)
                        hTe_out(b * SELS + e + 2)
                        act.wait_ge(scat[u], (b * (NE // 2) + i) * 16)
                        act.wait_ge(S["dn_ready"], b * NE + e + 1)
                        act.activation(ysc[u][0:CAP], PSF[0:CAP, 4 * 512:6 * 512], ACT.Copy, scale=gcol[u][0:CAP]).then_inc(S["y_ready"], 1)
            act.wait_ge(S["cnt_ready"], 1)
            most = act.value_load(cnt_i[0:1, 0:1], min_val=0, max_val=NT)
            experts(0)
            with act.Fori(1, PASSES) as b:
                with act.If(b * CAP < most):
                    experts(b)
            for t in range(NTILE):
                r = TROWS[t]
                act.wait_ge(S["fin_gb"], t + 1)
                act.activation(junk[0:r], yf[0:r, t, :], ACT.Square, accum_out=rms2[0:r, t:t + 1]).then_inc(S["fin_sq"], 1)
                act.wait_ge(S["fin_sq"], t + 1)
                act.activation(rms2[0:r, t:t + 1], rms2[0:r, t:t + 1], ACT.Sqrt, bias=eps_t[0:r], scale=1.0 / D).then_inc(S["fin_rs"], 1)

        @block.tensor
        def _(pe):
            used = [0]

            def free(j):
                if j < 2:
                    return
                if j - 2 < J_A:
                    pe.wait_ge(S["act_taken"], j - 1)
                else:
                    pe.wait_ge(S["dve_taken"], j - 1 - J_A)

            def project(j, lhs, rhs, nk, item=True, rows=P):
                free(j)
                if item:
                    n = used[0]
                    pe.wait_ge(w_full[n % 4], 16 * (n // 4 + 1))
                for a in range(2):
                    for k in range(nk):
                        mm = pe.matmul(PB[j % 2][0:rows, a, 0:HALF], lhs(k), rhs(k)[:, HALF * a:HALF * a + HALF],
                                       start=(k == 0), stop=(k == nk - 1))
                mm.then_inc(S["proj_done"], 1)
                used[0] += item

            def w(k):
                return wring[:, used[0] % 4, P * k:P * k + P]

            def hk(k):
                return hT[:, k, :]

            pe.wait_ge(S["ones_set"], 1)
            pe.wait_ge(S["cst_in"], 16)
            pe.wait_ge(S["sq_done"], KD)
            project(J_SS, lambda k: ones[:, :], lambda k: sq[:, k, :], KD, item=False)
            pe.wait_ge(S["h_done"], KD)
            for c in range(4):
                project(J_QI + c, w, hk, KD)
            project(J_KI, w, hk, KD)
            free(J_WI)
            pe.wait_ge(S["small_in"], 96)
            for t in range(NTILE):
                for k in range(KD):
                    mm = pe.matmul(PB[J_WI % 2][0:TROWS[t], 0, H * t:H * t + H], hT[:, k, P * t:P * t + TROWS[t]], wi_sb[:, k, :],
                                   start=(k == 0), stop=(k == KD - 1))
            mm.then_inc(S["proj_done"], 1)
            pe.wait_ge(S["act_taken"], J_KI + 1)
            for i, (t, h) in enumerate(DOTS):
                if i >= 2:
                    pe.wait_ge(S["relu_done"], i - 1)
                o = 64 * (h % 2)
                for a in range(0, KEYS[t], 512):
                    z = min(KEYS[t], a + 512)
                    mm = pe.matmul(AB[i % 2][0:ROWS[t], a:z], qiT[o:o + 64, h // 2, P * t:P * t + ROWS[t]], kiT[o:o + 64, a:z],
                                   start=True, stop=True)
                mm.then_inc(S["dots_ready"], 1)
            pe.wait_ge(S["relu_done"], len(DOTS))
            pe.wait_ge(S["zi_set"], 16 * 16)
            pe.wait_ge(S["kinew_set"], 2)
            pe.wait_ge(S["kidx_in"], 16 * NS * NPAGE)
            for a in range(3):
                lo, hi = 512 * a, min(KEYS_S, 512 * a + 512)
                for j in range(4):
                    mm = pe.matmul(PSF[0:64, 4 * 512 + lo:4 * 512 + hi], zi[:, 64 * j:64 * j + 64], kidx[:, j, lo:hi],
                                   start=(j == 0), stop=(j == 3))
            mm.then_inc(S["dots_ready"], 1)
            pe.wait_ge(S["relu_done"], len(DOTS) + 1)
            pe.wait_ge(S["wblk_done"], 1)
            for a in range(3):
                lo, hi = 512 * a, min(KEYS_S, 512 * a + 512)
                mm = pe.matmul(PSF[0:NS, 4 * 512 + lo:4 * 512 + hi], wblk[0:64], relu_s[0:64, lo:hi], start=True, stop=True)
            mm.then_inc(S["dots_ready"], 1)
            for c in range(4):
                project(J_K + c, w, hk, KD)
            for c in range(4):
                project(J_Q + c, w, hk, KD)

            def qk_sample(b):
                if b == 0:
                    pe.wait_ge(S["zq_done"], 2)
                    pe.wait_ge(S["sidx_taken"], 1)
                pe.wait_ge(kv_full[b % 2], 128 * (b // 2 + 1))
                for t in range(NPAGE):
                    for c in range(4):
                        mm = pe.matmul(L_s[:, t, 8 * b:8 * b + 8], kv[b % 2][:, t, P * c:P * c + P], zq[:, 64 * c + 8 * b:64 * c + 8 * b + 8],
                                       start=(c == 0), stop=(c == 3))
                mm.then_inc(S["kvu"], 1)
                for c in range(4):
                    mm = pe.matmul(L_n[0:NS, 8 * b:8 * b + 8], kT[:, c, NP_:NT], zq[:, 64 * c + 8 * b:64 * c + 8 * b + 8],
                                   start=(c == 0), stop=(c == 3))
                if b == NS - 1:
                    mm.then_inc(S["Lqk_done"], 1)

            for g in range(PG):
                project(J_P + g, w, hk, KD)
            pe.wait_ge(S["wv_in"], 16)
            for t in range(NTILE):
                free(J_V + t)
                for k in range(KD):
                    mm = pe.matmul(PB[(J_V + t) % 2][0:TROWS[t], 0, :], hT[:, k, P * t:P * t + TROWS[t]], w_v_sb[:, k, :],
                                   start=(k == 0), stop=(k == KD - 1))
                mm.then_inc(S["proj_done"], 1)
                qk_sample(t)
            for g in range(PG):
                pe.wait_ge(S["pool_done"], g + 1)
                project(J_MIX + g, lambda k: mix_sb[:, g, :], lambda k: pT[:, g, PAD:], 1, item=False)
                if NTILE + g < NS:
                    qk_sample(NTILE + g)
            pe.wait_ge(S["smask_done"], 1)
            pe.wait_ge(S["cst_in"], 16)
            for t in range(NPAGE):
                mm = pe.transpose(bank(7, NS, NS * t), score_s[0:NS, P * t:P * t + P], ident[0:NS, 0:NS])
            mm.then_inc(S["smT_ready"], 1)

            def sample_max():
                pe.wait_ge(S["lgs_done"], 1)
                pe.transpose(bank(6, P)[0:64], m_all, ident).then_inc(S["mxT_ready"], 1)
                pe.wait_ge(S["mdiag_done"], 1)
                pe.matmul(bank(6, 64, P), ones[0:64, :], dg[:, :], start=True, stop=True).then_inc(S["mb_ready"], 1)

            def sample_sums():
                pe.wait_ge(S["exps_done"], 1)
                for t in range(9):
                    mm = pe.matmul(bank(6, 64, 192), ones[:, :], lg_s[:, t, :], start=(t == 0), stop=(t == 8))
                mm.then_inc(S["sums_ready"], 1)

            def pv_sample(b):
                n = NS + b
                pe.wait_ge(kv_full[n % 2], 128 * (n // 2 + 1))
                if b == 0:
                    pe.wait_ge(S["vnew_in"], 16)
                for c in range(4):
                    for t in range(NPAGE):
                        mm = pe.matmul(PO[:, 64 * c + 8 * b:64 * c + 8 * b + 8], kv[n % 2][:, t, P * c:P * c + P], lg_s[:, t, 8 * b:8 * b + 8],
                                       start=(t == 0), stop=False)
                    mm2 = pe.matmul(PO[:, 64 * c + 8 * b:64 * c + 8 * b + 8], v_new[:, P * c:P * c + P], lg_s[0:NS, 8, 8 * b:8 * b + 8],
                                    start=False, stop=True)
                mm2.then_inc(S["kvu"], 1)

            pm = lambda k: pT[:, k, PAD:]
            for d in range(KD):
                j = J_GATE + 3 * d
                project(j, w, hk, KD)
                if d == 0:
                    pe.wait_ge(S["act_taken"], J_MIX + PG)
                project(j + 1, w, pm, PG)
                project(j + 2, w, hk, KD)
                if d == 0:
                    sample_max()
                if d == 1:
                    sample_sums()
                if d >= 1:
                    pv_sample(d - 1)
            pv_sample(NS - 1)

            def logits(i):
                t, h = HEADS[i]
                o = 64 * (h % 2)
                if i >= 2:
                    pe.wait_ge(S["lgp_done"], i - 1)
                for a in range(0, KEYS[t], 512):
                    z = min(KEYS[t], a + 512)
                    mm = pe.matmul(SB_[i % 2][0:ROWS[t], a:z], qT[o:o + 64, h // 2, P * t:P * t + ROWS[t]], kT[o:o + 64, h // 2, a:z],
                                   start=True, stop=True)
                mm.then_inc(S["s_ready"], 1)

            def turn(i):
                t, h = HEADS[i]
                r = ROWS[t]
                pe.wait_ge(S["exp_done"], i + 1)
                if i >= 2:
                    pe.wait_ge(S["pt_taken"], i - 1)
                for a in range(0, KEYS[t], P):
                    z = min(KEYS[t], a + P)
                    mm = pe.transpose(PTB[i % 2][0:z - a, a // P * r:a // P * r + r], lg[i % 3][0:r, a:z], ident[0:r, 0:r])
                mm.then_inc(S["pt_ready"], 1)

            def values(i):
                t, h = HEADS[i]
                r = ROWS[t]
                pe.wait_ge(S["pt_taken"], i + 1)
                if h == 0 and t:
                    pe.wait_ge(S["o_norm"], t)
                for a in range(0, KEYS[t], P):
                    z = min(KEYS[t], a + P)
                    mm = pe.matmul(O_p[0:r, HD * h:HD * h + HD], pt[i % 2][0:z - a, a // P * r:a // P * r + r],
                                   vN[0:z - a, a // P, HD * h:HD * h + HD], start=(a == 0), stop=(z == KEYS[t]))
                mm.then_inc(S["pv_head"], 1)

            def turn_out(t):
                pe.wait_ge(S["o_norm"], t + 1)
                pe.wait_ge(S["attn_s_done"], 2)
                if t:
                    pe.wait_ge(S["oT_taken"], t)
                r = ROWS[t]
                for c in range(4):
                    mm = pe.transpose(bank(5, r, r * c), o_sb[0:r, P * c:P * c + P], ident[0:r, 0:r])
                mm.then_inc(S["oT_ready"], 1)

            pe.wait_ge(S["act_taken"], J_A)
            pe.wait_ge(S["mdiag_done"], 3)
            logits(0)
            for i in range(len(HEADS)):
                if i + 1 < len(HEADS):
                    logits(i + 1)
                turn(i)
                if i:
                    values(i - 1)
                if HEADS[i][1] == 1 and HEADS[i][0]:
                    turn_out(HEADS[i][0] - 1)
            values(len(HEADS) - 1)
            turn_out(NTILE - 1)

            pe.wait_ge(S["oT_taken"], NTILE)
            pe.wait_ge(S["lgp_done"], len(HEADS))
            pe.wait_ge(S["pt_taken"], len(HEADS))
            for d in range(KD):
                project(J_A + d, w, lambda k: attnT[:, k, :], 4)
            pe.wait_ge(S["m_done"], KD)
            pe.wait_ge(S["wo0_in"], 16)
            pe.wait_ge(S["wo1_in"], 16)

            def hf_turn(t):
                j, r = J_TR + t, TROWS[t]
                if t < 2:
                    pe.wait_ge(S["dve_taken"], KD + NTILE - 1 + t)
                else:
                    pe.wait_ge(S["hfT_taken"], t - 1)
                pe.wait_ge(S["hf_done"], t + 1)
                for k in range(KD):
                    mm = pe.transpose(PSF[:, 1024 * (j % 2) + r * k:1024 * (j % 2) + r * k + r], hf(t)[0:r, P * k:P * k + P], ident[0:r, 0:r])
                mm.then_inc(S["hfT_ready"], 1)

            def route(t):
                r = TROWS[t]
                pe.wait_ge(S["hfT_taken"], t + 1)
                for k in range(KD):
                    mm = pe.matmul(bank(4, NE, NE * t)[0:r], hfT[t % 2][:, k, 0:r], wr_sb[:, k, :], start=(k == 0), stop=(k == KD - 1))
                mm.then_inc(S["router_ready"], 1)

            for t in range(NTILE):
                j, r = J_WO + t, TROWS[t]
                free(j)
                for a in range(2):
                    for k in range(KD):
                        mm = pe.matmul(PB[j % 2][0:r, a, :], sga[:, k, P * t:P * t + r], wo[a][:, k, :], start=(k == 0), stop=(k == KD - 1))
                mm.then_inc(S["proj_done"], 1)
            for t in range(NTILE):
                hf_turn(t)
                if t:
                    route(t - 1)
            route(NTILE - 1)
            pe.wait_ge(S["m_ready"], 1)
            for t in range(NTILE):
                for s in range(t + 1):
                    mm = pe.matmul(bank(6, NE, NE * t), tri if s == t else ones[:, :], rt_m[:, s, :], start=(s == 0), stop=(s == t))
            for s in range(NTILE):
                mm = pe.matmul(bank(6, NE, NE * NTILE), ones[:, :], rt_m[:, s, :], start=(s == 0), stop=(s == NTILE - 1))
            mm.then_inc(S["rank_ready"], 1)
            pe.wait_ge(S["gtr_ready"], 1)
            for t in range(4):
                pe.transpose(bank(7, P, P * t)[0:NE], rt_g[:, t, :], ident)
            pe.transpose(bank(5, P)[0:NE], rt_g[:, 4, :], ident).then_inc(S["gtr_ready"], 1)

            def pick(n, e, u):
                pe.wait_ge(S["cmp_ready"], n)
                for t in range(NTILE):
                    mm = pe.matmul(bank(6, 3, 8 * u)[0:CAP], cmpm[u][:, t, :], gx[:, t, bass.ds(e, 1), :].rearrange("p a x -> p (a x)"),
                                   start=(t == 0), stop=(t == NTILE - 1))
                mm.then_inc(S["slot_ready"], 1)

            def turn_rows(n, half, u):
                pe.wait_ge(gath[u], half * 16)
                for k in range(KD):
                    mm = pe.transpose(bank(2 + k // 4, CAP, CAP * (k % 4)), xg[u][0:CAP, P * k:P * k + P], ident[0:CAP, 0:CAP])
                mm.then_inc(S["xt_ready"], 1)

            def experts(b):
                pick(b * SELS + 1, 0, 0)
                turn_rows(b * SELS + 1, b * (NE // 2 + 1) + 1, 0)
                with pe.Fori(0, NE // 2) as i:
                    for u in range(2):
                        e = i * 2 + u
                        ne = b * NE + e
                        for c in range(CHUNKS):
                            pe.wait_ge(r_full[c], (ne + 1) * 16)
                            if c == 0:
                                pe.wait_ge(S["hTe_ready"], b * SELS + e + 1)
                            pe.wait_ge(S["gu_taken"], ne * CHUNKS + c + 1)
                            wc = W6[:, slot(c):slot(c + 1)].rearrange("p (k f x) -> p k f x", k=KD, f=4)
                            for f in range(4):
                                for k in range(KD):
                                    mm = pe.matmul(bank(c % 2, CAP, CAP * f), wc[:, k, f, :], hTe[:, k, :], start=(k == 0), stop=(k == KD - 1))
                            mm.then_inc(S["gu_ready"], 1)
                            if c == 1:
                                pick(b * SELS + e + 2, e + 1, 1 - u)
                        if u == 0:
                            turn_rows(b * SELS + e + 2, b * (NE // 2) + i + 1, 1)
                        else:
                            turn_rows(b * SELS + e + 2, b * (NE // 2 + 1) + i + 2, 0)
                        pe.wait_ge(S["y_ready"], ne)
                        for f in range(KD):
                            if f % 4 == 0:
                                pe.wait_ge(r_full[CHUNKS + f // 4], (ne + 1) * 16)
                            if f % 2 == 0:
                                pe.wait_ge(S["act_ready"], ne * CHUNKS + f // 2 + 1)
                            for a in range(2):
                                mm = pe.matmul(PSF[0:CAP, (4 + a) * 512:(5 + a) * 512], actT[:, f, :],
                                               W6[:, slot(4) + D * f + 512 * a:slot(4) + D * f + 512 * a + 512],
                                               start=(f == 0), stop=(f == KD - 1))
                            if f == 3:
                                mm.then_inc(S["dn_half"], 1)
                        mm.then_inc(S["dn_ready"], 1)

            pe.wait_ge(S["cnt_ready"], 1)
            most = pe.value_load(cnt_i[0:1, 0:1], min_val=0, max_val=NT)
            experts(0)
            with pe.Fori(1, PASSES) as b:
                with pe.If(b * CAP < most):
                    experts(b)
            pe.wait_ge(S["all_added"], 1)
            pe.wait_ge(S["bd_in"], 16)
            pe.wait_ge(S["gT_done"], 1)
            for t in range(NTILE):
                if t >= 2:
                    pe.wait_ge(S["fin_gb"], t - 1)
                for a in range(2):
                    mm = pe.matmul(PB[t % 2][0:TROWS[t], a, :], gT[0:NE, t, 0:TROWS[t]], bd_sb[0:NE, 512 * a:512 * a + 512], start=True, stop=True)
                mm.then_inc(S["gb_ready"], 1)

        @block.vector
        def _(dve):
            n = [0]
            L = lambda ins: link(dve, ins, "dve_step", n)
            dve.wait_ge(S["act_taken"], 1)
            L(dve.reciprocal(KI[:, :], KI[:, :]))
            dve.wait_ge(S["gmix_in"], 16)
            for k in range(KD):
                dve.scalar_tensor_tensor(out=hT[:, k, :], in0=x_in[:, k, :], scalar=gmix_sb[:, k:k + 1], in1=KI[:, :],
                                         op0=ALU.mult, op1=ALU.mult).then_inc(S["h_done"], 1)
            dve.wait_ge(S["act_taken"], J_WI + 1)
            for i, (t, h) in enumerate(DOTS):
                dve.wait_ge(S["relu_done"], i + 1)
                r, w = ROWS[t], KEYS[t]
                sc = score[0:r, SCORE_AT[t]:SCORE_AT[t] + w]
                rl = relu_p[i % 2][0:r, 0:w]
                if h == 0:
                    dve.tensor_scalar(sc, rl, wi_nat[0:r, t, h:h + 1], None, ALU.mult).then_inc(S["acc_done"], 1)
                else:
                    dve.wait_ge(S["acc_done"], i)
                    dve.scalar_tensor_tensor(out=sc, in0=rl, scalar=wi_nat[0:r, t, h:h + 1], in1=sc,
                                             op0=ALU.mult, op1=ALU.add).then_inc(S["acc_done"], 1)
            dve.wait_ge(S["dots_ready"], len(DOTS) + 2)
            dve.tensor_copy(score_s[0:NS], PSF[0:NS, 4 * 512:4 * 512 + KEYS_S]).then_inc(S["sidx_taken"], 1)
            dve.wait_ge(S["sidx_taken"], 1)

            def top(sc, rows, k):
                for _ in range(k // 8):
                    L(dve.max(out=max8[0:rows], in_=sc))
                    L(dve.match_replace(out=sc, in_to_replace=max8[0:rows], in_values=sc, imm_value=TAKEN))
            top(score_s[0:NS], NS, TOPK_S)
            dve.tensor_scalar(score_s[0:NS], score_s[0:NS], (NONCAUSAL + TAKEN) / 2, OUT, ALU.is_gt, ALU.mult).then_inc(S["smask_done"], 1)
            dve.wait_ge(S["smask_done"], 1)
            dve.wait_ge(S["cst_in"], 16)
            L(dve.scalar_tensor_tensor(out=maskT[0:NS, 8, :], in0=ident[0:NS, 0:NS], scalar=score_s[0:NS, PAST:KEYS_S], in1=offd,
                                       op0=ALU.mult, op1=ALU.add))
            dve.wait_ge(S["smT_ready"], 1)
            L(dve.tensor_copy(maskT[:, 0:8, :], bank(7, 64)))
            dve.wait_ge(S["Lqk_done"], 1)
            dve.wait_ge(S["zero_set"], 2)
            dve.wait_ge(S["small_in"], 96)

            def v4(ap):
                return ap.rearrange("p t (b h) -> p t b h", h=H)

            def per_seq(ap, t):
                return ap.unsqueeze(3).broadcast_to([ap.shape[0], t, NS, H])

            def per_head(ap, t):
                return ap.unsqueeze(2).broadcast_to([ap.shape[0], t, NS, H])
            L(dve.tensor_tensor(v4(lg_s[:, 0:8, :]), v4(L_s), per_seq(maskT[:, 0:8, :], 8), ALU.add))
            L(dve.tensor_tensor(v4(lg_s[0:NS, 8:9, :]), v4(L_n[0:NS].unsqueeze(1)), per_seq(maskT[0:NS, 8:9, :], 1), ALU.add))
            L(dve.tensor_tensor(v4(lg_s[:, 0:8, :]), v4(lg_s[:, 0:8, :]), per_head(bias_sb[:, 0:8, :], 8), ALU.add))
            L(dve.tensor_tensor(v4(lg_s[0:NS, 8:9, :]), v4(lg_s[0:NS, 8:9, :]), per_head(bias_sb[0:NS, 8:9, :], 1), ALU.add))
            dve.tensor_reduce(m_all, lg_s[:, :, :].rearrange("p t x -> p x t"), AX.X, ALU.max).then_inc(S["lgs_done"], 1)
            dve.wait_ge(S["mxT_ready"], 1)
            L(dve.tensor_reduce(m64[0:64], bank(6, P)[0:64], AX.X, ALU.max))
            dve.tensor_scalar(dg[:, :], ident[0:64, 0:64], m64[0:64], None, ALU.mult).then_inc(S["mdiag_done"], 1)
            dve.wait_ge(S["mb_ready"], 1)
            dve.tensor_tensor(lg_s[:, :, :], lg_s[:, :, :], bank(6, 64, P).unsqueeze(1).broadcast_to([P, 9, 64]), ALU.subtract)\
                .then_inc(S["mdiag_done"], 1)

            def top_tile(t):
                r, w = ROWS[t], KEYS[t]
                sc = score[0:r, SCORE_AT[t]:SCORE_AT[t] + w]
                dve.wait_ge(S["causal_done"], 5 - t)
                top(sc, r, TOPK_P)
                dve.tensor_scalar(sc, sc, (NONCAUSAL + TAKEN) / 2, OUT, ALU.is_gt, ALU.mult).then_inc(S["mask_done"], 1)
            top_tile(1)
            dve.wait_ge(S["sums_ready"], 1)
            dve.reciprocal(rs_s[:, :], bank(6, 64, 192)).then_inc(S["mdiag_done"], 1)
            for t in (2, 3, 4):
                top_tile(t)
            dve.wait_ge(S["mdiag_done"], 3)
            dve.wait_ge(S["kvu"], 2 * NS)
            pov = PO.rearrange("p (c x) -> p c x", x=66)
            rsv = rs_s[:, :].rearrange("p (b h) -> p h b", h=H)
            for hp in range(2):
                lo = 64 * hp
                dve.tensor_tensor(attnT[lo:lo + 64, :, NP_:NT], pov[lo:lo + 64, :, hp:hp + 64:8], rsv[lo:lo + 64, hp::2, :], ALU.mult)\
                    .then_inc(S["attn_s_done"], 1)

            def norm_out(t):
                r = ROWS[t]
                dve.wait_ge(S["exp_done"], H * (t + 1))
                L(dve.reciprocal(rsum[0:r, H * t:H * t + H], esum[0:r, H * t:H * t + H]))
                dve.wait_ge(S["pv_head"], H * (t + 1))
                if t:
                    dve.wait_ge(S["oT_ready"], t)
                dve.tensor_tensor(o_sb[0:r].rearrange("p (h d) -> p h d", h=H), O_p[0:r].rearrange("p (h d) -> p h d", h=H),
                                  rsum[0:r, H * t:H * t + H].unsqueeze(2).broadcast_to([r, H, HD]), ALU.mult).then_inc(S["o_norm"], 1)
            for i, (t, h) in enumerate(HEADS):
                r, w = ROWS[t], KEYS[t]
                dve.wait_ge(S["s_ready"], i + 1)
                dve.wait_ge(S["mb_done"], i + 1)
                if i >= 3:
                    dve.wait_ge(S["pt_ready"], i - 2)
                dve.tensor_tensor_reduce(lg[i % 3][0:r, 0:w], SB_[i % 2][0:r, 0:w], mb[i % 2][0:r, 0:w], -1.0, 3.0e38,
                                         ALU.add, ALU.min, nmax[0:r, i:i + 1]).then_inc(S["lgp_done"], 1)
                if h == 1 and t:
                    norm_out(t - 1)
            norm_out(NTILE - 1)
            dve.wait_ge(S["b_mult"], KD)
            for d in range(KD):
                j = J_A + d
                dve.wait_ge(S["proj_done"], j + 1)
                m = sga[:, d, :].rearrange("p (a b) -> p a b", a=2)
                dve.tensor_tensor(m, PB[j % 2][:, :, 0:HALF], m, ALU.mult).then_inc(S["dve_taken"], 1)
                dve.wait_ge(S["dve_taken"], d + 1)
                dve.tensor_tensor(sga[:, d, :], sga[:, d, :], sbb[:, d, :], ALU.add).then_inc(S["m_done"], 1)
            def norm_rows(t):
                r = TROWS[t]
                dve.wait_ge(S["row_ms"], 2 * t + 2)
                L(dve.reciprocal(rms[0:r, t:t + 1], rms[0:r, t:t + 1]))
                dve.scalar_tensor_tensor(out=hf(t)[0:r], in0=xn(t)[0:r], scalar=rms[0:r, t:t + 1], in1=gffn[0:r],
                                         op0=ALU.mult, op1=ALU.mult).then_inc(S["hf_done"], 1)
            dve.wait_ge(S["xn_in"], 16 * NTILE)
            for t in range(NTILE):
                j, r = J_WO + t, TROWS[t]
                dve.wait_ge(S["proj_done"], j + 1)
                x1 = xn(t)[0:r].rearrange("p (a b) -> p a b", a=2)
                dve.tensor_tensor(x1, PB[j % 2][0:r], x1, ALU.add).then_inc(S["dve_taken"], 1)
                if t == 0:
                    dve.wait_ge(S["late_in"], 48)
                if t:
                    norm_rows(t - 1)
            norm_rows(NTILE - 1)
            dve.wait_ge(S["router_ready"], NTILE)
            L(dve.memset(rt_log, 0.0))
            L(dve.tensor_tensor(rt_log[:, 0:4, :], bank(4, 4 * NE).rearrange("p (t e) -> p t e", t=4), rt_br.unsqueeze(1).broadcast_to([P, 4, NE]), ALU.add))
            L(dve.tensor_tensor(rt_log[0:TAIL, 4, :], bank(4, NE, 4 * NE)[0:TAIL], rt_br[0:TAIL], ALU.add))
            for t in range(NTILE):
                L(dve.max(out=top_v[:, t, :], in_=rt_log[:, t, :]))
                L(dve.max_index(out=top_i[:, t, :], in_max=top_v[:, t, :], in_values=rt_log[:, t, :]))
            L(dve.tensor_copy(rt_e, top_i[:, :, :]))
            dve.tensor_tensor(rt_w, top_v[:, :, 0:TOPE], top_v[:, :, 0:1].broadcast_to([P, NTILE, TOPE]), ALU.subtract).then_inc(S["sel_ready"], 1)
            L(dve.tensor_tensor(rt_eq, iota_e.unsqueeze(1).unsqueeze(1).broadcast_to([P, NTILE, TOPE, NE]),
                                rt_e[:, :, 0:TOPE].unsqueeze(3).broadcast_to([P, NTILE, TOPE, NE]), ALU.is_equal))
            L(dve.tensor_reduce(rt_m, rt_eq.rearrange("p t k e -> p t e k"), AX.X, ALU.add))
            dve.tensor_tensor(rt_m[:, 4, :], rt_m[:, 4, :], valid.broadcast_to([P, NE]), ALU.mult)\
                .then_inc(S["m_ready"], 1)
            dve.wait_ge(S["sel_ready"], 2)
            L(dve.tensor_reduce(sum4, rt_w, AX.X, ALU.add))
            L(dve.reciprocal(sum4, sum4))
            L(dve.tensor_tensor(rt_w, rt_w, sum4.unsqueeze(2).broadcast_to([P, NTILE, TOPE]), ALU.mult))
            L(dve.tensor_tensor(rt_eg, rt_eq, rt_w.unsqueeze(3).broadcast_to([P, NTILE, TOPE, NE]), ALU.mult))
            dve.tensor_reduce(rt_g, rt_eg.rearrange("p t k e -> p t e k"), AX.X, ALU.add).then_inc(S["gtr_ready"], 1)
            dve.wait_ge(S["gtr_ready"], 1)
            dve.wait_ge(S["hfT_ready"], NTILE)
            dve.wait_ge(S["acc_init"], 16 * 2 * NTILE)
            L(dve.memset(posv, -1.0))
            L(dve.memset(gx, 0.0))
            L(dve.tensor_copy(gx[:, :, 0:NE, 0], tokid.unsqueeze(2).broadcast_to([P, NTILE, NE])))
            L(dve.memset(gx[:, :, 0:NE, 1], 1.0))
            L(dve.tensor_copy(gx[:, :, 0:NE, 2], rt_g))
            dve.wait_ge(S["m_ready"], 1)
            dve.wait_ge(S["rank_ready"], 1)
            L(dve.scalar_tensor_tensor(out=rt_eg[:, :, 0, :], in0=bank(6, NTILE * NE).rearrange("p (t e) -> p t e", t=NTILE), scalar=1.0, in1=rt_m,
                                       op0=ALU.add, op1=ALU.mult))
            L(dve.tensor_scalar(posv[:, :, 0:NE], rt_eg[:, :, 0, :], -1.0, None, ALU.add))
            L(dve.tensor_reduce(rt_cnt[0:1, 0:1], bank(6, NE, NE * NTILE)[0:1], AX.X, ALU.max))
            L(dve.tensor_copy(cnt_i[0:1, 0:1], rt_cnt[0:1, 0:1]))
            L(dve.tensor_copy(iota_b[:, :], iota96))
            dve.wait_ge(S["gtr_ready"], 2)
            L(dve.tensor_copy(gT[0:NE, 0:4, :], bank(7)[0:NE].rearrange("p (t x) -> p t x", t=4)))
            dve.tensor_copy(gT[0:NE, 4, :], bank(5, P)[0:NE]).then_inc(S["gT_done"], 1)
            dve.wait_ge(S["gT_done"], 1)
            dve.sem_inc(S["cnt_ready"], 1)
            dve.wait_ge(S["bgu_in"], 16)
            dve.sem_inc(S["gu_taken"], 2)

            def compare(e, u):
                dve.tensor_tensor(cmpm[u], iota_b[:, :].unsqueeze(1).broadcast_to([P, NTILE, CAP]),
                                  posv[:, :, bass.ds(e, 1)].broadcast_to([P, NTILE, CAP]), ALU.is_equal).then_inc(S["cmp_ready"], 1)

            def index(nsel, u):
                dve.wait_ge(S["slot_ready"], nsel)
                sl = bank(6, 3, 8 * u)[0:CAP]
                dve.scalar_tensor_tensor(out=unused[u][0:CAP], in0=trash[0:CAP], scalar=sl[:, 1:2], in1=trash[0:CAP], op0=ALU.mult, op1=ALU.subtract)\
                    .then_inc(S["unused_done"], 1)
                dve.wait_ge(S["unused_done"], nsel)
                dve.tensor_tensor(idx_i[u][0:CAP, :], sl[:, 0:1], unused[u][0:CAP], ALU.subtract)
                dve.tensor_copy(gcol[u][0:CAP], sl[:, 2:3]).then_inc(S["idx_ready"], 1)

            def experts(b):
                compare(0, 0)
                index(b * SELS + 1, 0)
                with dve.Fori(0, NE // 2) as i:
                    for u in range(2):
                        e = i * 2 + u
                        ne = b * NE + e
                        compare(e + 1, 1 - u)
                        for c in range(CHUNKS):
                            nc_ = ne * CHUNKS + c
                            if c == 2:
                                if u == 0:
                                    dve.wait_ge(scat[1], (b * (NE // 2) + i) * 16)
                                else:
                                    dve.wait_ge(scat[0], (b * (NE // 2) + i + 1) * 16)
                                index(b * SELS + e + 2, 1 - u)
                            dve.wait_ge(S["gu_ready"], nc_ + 1)
                            t_ = gu_t[c % 2]
                            dve.tensor_tensor(t_, bank(c % 2, 4 * CAP).rearrange("p (f s) -> p f s", f=4),
                                              b_gu_sb[:, bass.ds(e, 1), 4 * c:4 * c + 4].rearrange("p a f -> p (a f)").unsqueeze(2).broadcast_to([P, 4, CAP]),
                                              ALU.add).then_inc(S["gu_taken"], 1)
                            dve.wait_ge(S["gu_taken"], nc_ + 3)
                            dve.tensor_scalar(t_[:, 0:2, :], t_[:, 0:2, :], 7.0, None, ALU.min).then_inc(S["clamp_done"], 1)
                            dve.tensor_scalar(t_[:, 2:4, :], t_[:, 2:4, :], 7.0, -7.0, ALU.min, ALU.max).then_inc(S["up_done"], 1)
                            dve.wait_ge(S["clamp_done"], nc_ + 1)
                            dve.wait_ge(S["sig_done"], nc_ + 1)
                            dve.tensor_tensor(gs_t, t_[:, 0:2, :], sg_t[c % 2], ALU.mult).then_inc(S["gated"], 1)
                            dve.wait_ge(S["up_done"], nc_ + 1)
                            dve.wait_ge(S["gated"], nc_ + 1)
                            dve.scalar_tensor_tensor(out=actT[:, 2 * c:2 * c + 2, :], in0=t_[:, 2:4, :], scalar=1.0, in1=gs_t,
                                                     op0=ALU.add, op1=ALU.mult).then_inc(S["act_ready"], 1)

            most = dve.value_load(cnt_i[0:1, 0:1], min_val=0, max_val=NT)
            experts(0)
            with dve.Fori(1, PASSES) as b:
                with dve.If(b * CAP < most):
                    dve.tensor_scalar(iota_b[:, :], iota_b[:, :], float(CAP), None, ALU.add).then_inc(S["slots_moved"], 1)
                    dve.wait_ge(S["slots_moved"], b)
                    experts(b)
            def fin_row(t):
                r = TROWS[t]
                dve.wait_ge(S["fin_rs"], t + 1)
                L(dve.reciprocal(rms2[0:r, t:t + 1], rms2[0:r, t:t + 1]))
                dve.scalar_tensor_tensor(out=yf[0:r, t, :], in0=yf[0:r, t, :], scalar=rms2[0:r, t:t + 1], in1=gfin[0:r],
                                         op0=ALU.mult, op1=ALU.mult).then_inc(S["fin_y"], 1)
            dve.wait_ge(S["yf_in"], 32)
            for t in range(NTILE):
                r = TROWS[t]
                dve.wait_ge(S["gb_ready"], t + 1)
                y2 = yf[0:r, t, :].rearrange("p (a b) -> p a b", a=2)
                dve.tensor_tensor(y2, PB[t % 2][0:r], y2, ALU.add).then_inc(S["fin_gb"], 1)
                if t:
                    fin_row(t - 1)
            fin_row(NTILE - 1)


def constants():
    c = np.zeros((P, C_W), np.float32)
    i = np.arange(P)
    c[:, C_ID:C_ID + P] = np.eye(P)
    c[:, C_TRI:C_TRI + P] = i[:, None] < i[None, :]
    c[:, C_IOTA:C_IOTA + CAP] = np.arange(CAP)
    c[:, C_EXP:C_EXP + NE] = np.arange(NE)
    c[:, C_TOK:C_TOK + NTILE] = i[:, None] + P * np.arange(NTILE)
    c[:, C_TRASH] = NT + i
    for g in range(PG):
        c[:, C_RCNT + 16 * g:C_RCNT + 16 * g + 16] = 1.0 / np.minimum(np.arange(16) + 1, 2 << g)
    c[:, C_OFFD:C_OFFD + NS] = np.where(i[:, None] == np.arange(NS), 0.0, OUT)
    c[:, C_WSEL:C_WSEL + NS] = i[:, None] // H == np.arange(NS)
    c[:, C_VALID] = i < TAIL
    return c


def buckets(dist):
    n = np.maximum(dist, 0)
    exact = NB // 2
    large = exact + (np.log(np.maximum(n, 1) / exact) / np.log(128 / exact) * (NB - exact)).astype(np.int64)
    return np.where(n < exact, n, np.minimum(large, NB - 1))


def kernel(**inputs):
    import concourse.bacc as bacc
    from concourse.bass_utils import run_bass_kernel_spmd

    x = {k: np.asarray(v) for k, v in inputs.items()}
    rows = np.concatenate([x["meta_tokens"], x["x_prompt"][0], x["x_sample"][:, 0]], axis=0)
    w_in = x["w_in"][0]
    q, k, v, qi, ki, wi, p, ga, gb = np.split(w_in, np.cumsum([AW, AW, AW, AW, HD, H, AW, D, D])[:-1], axis=1)

    def tiles(w):
        return w.reshape(KD, P, -1, P).transpose(2, 1, 0, 3)
    gates = np.stack([tiles(gb), tiles(ga)], axis=1).reshape(2 * KD, P, KD, P)
    w_mt = np.concatenate([tiles(qi), tiles(np.concatenate([ki, ki], axis=1)), tiles(k), tiles(q), tiles(p), gates])

    def rows4(w):
        return w.reshape(4, P, KD, P).transpose(2, 1, 0, 3).reshape(KD, P, 512)
    i = np.arange(P)
    strip = x["rel_bias"][buckets(512 + i[:, None] - np.arange(STRIP)[None, :])].transpose(0, 2, 1)
    dist = np.concatenate([PAST - (i[:, None] + P * np.arange(NPAGE)[None, :]), np.zeros((P, 1), np.int64)], axis=1)
    arrays = {
        "xT": rows.T.reshape(KD, P, NT).transpose(1, 0, 2),
        "xnat": rows,
        "consts": constants(),
        "g_mix": x["g_mix"][0].reshape(KD, P).T,
        "w_mt": w_mt.reshape(-1, P, KD * P),
        "w_wi": wi.reshape(KD, P, H).transpose(1, 0, 2),
        "w_v": v.reshape(KD, P, AW).transpose(1, 0, 2),
        "w_mix": x["w_pool_mix"][0].transpose(1, 0, 2),
        "pool_scale": x["pool_scale"][0].reshape(PG, P).T,
        "w_bra": rows4(x["w_br_attn"][0]),
        "w_brp": rows4(x["w_br_pool"][0]),
        "w_out": x["w_out"][0].reshape(KD, P, 2, 512).transpose(2, 1, 0, 3),
        "w_router": x["w_router"][0].reshape(KD, P, NE).transpose(1, 0, 2),
        "b_router": x["b_router"][0],
        "b_gu": x["b_gate_up"][0].reshape(NE, 2, CHUNKS, 2, P).transpose(4, 0, 2, 1, 3).reshape(P, NE, 16),
        "w_gu": x["w_gate_up"][0].reshape(NE, KD, P, 2, CHUNKS, 2, P).transpose(0, 4, 2, 1, 3, 5, 6).reshape(NE, CHUNKS, P, RING),
        "w_down": x["w_down"][0].reshape(NE, 2, 4, P, D).transpose(0, 1, 3, 2, 4).reshape(NE, 2, P, RING),
        "b_down": x["b_down"][0],
        "g_ffn": x["g_ffn"][0],
        "g_final": x["g_final"],
        "bias_strip": strip,
        "bias_s": x["rel_bias"][buckets(dist)],
        "cache_kT": x["cache_k"][0].reshape(NPOOL, PAGE, 4, P).transpose(0, 3, 2, 1).reshape(NPOOL, P, 4 * PAGE),
        "cache_v": x["cache_v"][0].reshape(NPOOL, PAGE, AW),
        "cache_kiT": x["cache_kidx"][0].transpose(0, 2, 1),
        "page_table": x["page_table"].reshape(1, NS * NPAGE),
        "state": x["state_pool"][0],
        "stateT": x["state_pool"][0].reshape(NS, 15, PG, P).transpose(3, 2, 0, 1).reshape(P, PG * NS, 15),
    }
    outs = [("o_y", (NT, D)), ("o_kT", (P, 4, NT)), ("o_v", (NT, AW)), ("o_kiT", (HD, NT)), ("o_pT", (P, PG, 23)),
            ("o_state", (NS, 14, AW))]
    nc = bacc.Bacc("TRN2", target_bir_lowering=False, num_devices=1)
    args, feed = [], {}
    for name, a in arrays.items():
        a = np.ascontiguousarray(a)
        feed[name] = a
        args.append(nc.dram_tensor(name, a.shape, mybir.dt.from_np(a.dtype), kind="ExternalInput").ap())
    for name, shape in outs:
        args.append(nc.dram_tensor(name, shape, F32, kind="ExternalOutput").ap())
    build_step(nc, *args)
    r = run_bass_kernel_spmd(nc, [feed], core_ids=[0]).results[0]
    y = r["o_y"]
    kk = r["o_kT"].transpose(2, 1, 0).reshape(NT, H, HD)
    vv = r["o_v"].reshape(NT, H, HD)
    kki = r["o_kiT"].T
    pp = r["o_pT"].transpose(2, 1, 0).reshape(23, AW)
    new_pool = np.concatenate([r["o_state"], pp[15:, None]], axis=1)
    return (y[META:NP_][None], y[NP_:][:, None], kk[:NP_][None, None], vv[:NP_][None, None], kki[:NP_][None, None],
            pp[:15][None, None], kk[NP_:][None, :, None], vv[NP_:][None, :, None], kki[NP_:][None, :, None], new_pool[None])
```

```python
from contextlib import ExitStack

import concourse.bass as bass
import numpy as np
from concourse import mybir

F32 = mybir.dt.float32
F32R = mybir.dt.float32r
I32 = mybir.dt.int32
U32 = mybir.dt.uint32
ALU = mybir.AluOpType
ACT = mybir.ActivationFunctionType
AX = mybir.AxisListType
POOL = mybir.EngineType.Pool
SP = mybir.EngineType.SP

P = 128
D = 1024
KD = D // P
META, SEQ, NS = 16, 512, 8
NP_ = META + SEQ
NT = NP_ + NS
HALF = NT // 2
NTILE = 5
TAIL = NT - 4 * P
H, HD = 8, 64
AW = H * HD
PAGE, NPAGE, NPOOL = 128, 8, 80
PAST = PAGE * NPAGE
KEYS_S = PAST + 1
TOPK_P = min(256, SEQ // 4)
TOPK_S = min(256, KEYS_S // 4)
NB = 32
PG = 4
NE, TOPE = 32, 4
CAP = 96
PASSES = -(-NT // CAP)
SELS = NE + 1
CHUNKS = 4
STRIP = 640
OUT = -1.0e30
NONCAUSAL = -3.0e38
TAKEN = -3.3e38
EPS = 1e-6
PAD = 16

RING = 4096
KEYS = [min(P * (t + 1), NP_) for t in range(NTILE)]
ROWS = [P, P, P, P, META]
TROWS = [P, P, P, P, TAIL]
SCORE_AT = {1: 0, 2: 256, 3: 640, 4: 1152}
SCORE_W = 1680

C_ID, C_TRI, C_IOTA, C_EXP, C_TOK, C_TRASH, C_RCNT, C_WSEL, C_VALID, C_SELG, C_G32, C_SELM, C_H8, C_W = \
    0, 128, 256, 352, 384, 389, 390, 454, 462, 463, 527, 655, 659, 667


def build_step(nc, xT, xnat, consts, g_mix, w_mt, w_wi, w_v, w_mix, pool_scale, w_bra, w_brp, w_out,
               w_router, b_router, b_gu, w_gu, w_down, b_down, g_ffn, g_final, bias_strip, bias_s, bias_n,
               cache_kT, cache_v, cache_kiT, page_table, state, stateT,
               o_y, o_kT, o_v, o_kiT, o_pT, o_state):
    ctx = ExitStack()
    with ctx:
        def sb(name, shape, dt=F32):
            return ctx.enter_context(nc.sbuf_tensor(name, shape, dt))

        def sem(name):
            return ctx.enter_context(nc.semaphore(name))

        def dram(name, shape, dt=F32):
            return nc.dram_tensor(name, shape, dt).ap()

        y_acc = dram("y_acc", (NT + CAP, D))
        h_rows = dram("h_rows", (NT + CAP, D))
        wi_row = dram("wi_row", (NS, H))

        W6 = sb("weight_ring", [P, 6 * RING])
        X1 = sb("region_x1", [P, KD * NT])
        X2 = sb("region_x2", [P, KD * NT])
        KI = sb("region_ki", [P, NT])
        WR = sb("region_w", [P, 4 * 1024])
        cst = sb("cst", [P, C_W])
        ones = sb("ones", [P, P])
        wr_sb = sb("wr_sb", [P, KD, NE])
        smalls = sb("smalls", [P, 212])

        mx2 = sb("mx2", [P, 2])[:, :]
        nmx2 = sb("nmx2", [P, 2])[:, :]
        es2 = sb("es2", [P, 2])[:, :]
        rs2 = sb("rs2", [P, 2])[:, :]
        mq = sb("mq", [2, 32])[:, :]
        mq4 = sb("mq4", [2, P])[:, :]
        dnew = sb("dnew", [32, 2, 32])[:, :, :]
        bias_new = sb("bias_new", [P, 1])[:, :]
        idx_i = [sb(f"idx_i{n}", [P, 1], I32) for n in range(2)]
        cnt_i = sb("cnt_i", [1, 8], I32)
        pt_sb = sb("pt_sb", [1, NS * NPAGE], I32)
        choices = sb("choices", [P, NTILE * SELS * 3])
        with ExitStack() as early:
            HR, QK, QI, VN = [early.enter_context(nc.sbuf_tensor(name, [P, n], F32)) for name, n in
                              (("region_h", KD * NT), ("region_qk", 8 * NT), ("region_qi", 4 * NT), ("region_v", NTILE * AW))]
        XR = sb("region_experts", [P, 3360])
        w_hi = sb("down_hi", [P, 4, D], F32R)
        w_lo = sb("down_lo", [P, 4, D], F32R)
        act_hi = sb("act_hi", [P, KD, CAP], F32R)
        act_lo = sb("act_lo", [P, KD, CAP], F32R)

        def part(region, at, *shape):
            n = int(np.prod(shape))
            v = region[:, at:at + n]
            names = "abcd"[:len(shape)]
            if len(shape) == 1:
                return v
            return v.rearrange(f"p ({' '.join(names)}) -> p {' '.join(names)}", **dict(zip(names[1:], shape[1:])))

        def slot(n):
            return n * RING

        ident = cst[:, C_ID:C_ID + P]
        tri = cst[:, C_TRI:C_TRI + P]
        iota96 = cst[:, C_IOTA:C_IOTA + CAP]
        iota_e = cst[:, C_EXP:C_EXP + NE]
        tokid = cst[:, C_TOK:C_TOK + NTILE]
        trash = cst[:, C_TRASH:C_TRASH + 1]
        rcnt = cst[:, C_RCNT:C_RCNT + 64].rearrange("p (g t) -> p g t", g=PG)
        selg = cst[0:NS, C_SELG:C_SELG + 64].rearrange("b (g x) -> b g x", g=2)
        same32 = cst[:, C_G32:C_G32 + P]
        selm = cst[:, C_SELM:C_SELM + 4]
        head8 = cst[:, C_H8:C_H8 + H]
        wsel = cst[0:64, C_WSEL:C_WSEL + NS]
        valid = cst[:, C_VALID:C_VALID + 1]

        x_in = part(X1, 0, KD, NT)
        sq = part(X2, 0, KD, NT)
        hT = part(X1, 0, KD, NT)
        qT = part(QK, 0, 4, NT)
        kT = part(QK, 4 * NT, 4, NT)
        qi_v = [part(QI, 0, 4, NT), part(W6, 0, 4, NT)]
        attnT = part(X1, 0, 4, NT)
        kiT = KI[:, :]
        vN = part(VN, 0, NTILE, AW)
        wring = part(WR, 0, 4, 1024)
        w_v_sb = part(W6, slot(5), KD, AW)
        kv = [part(W6, slot(n), NPAGE, AW) for n in range(2)]
        pT = part(W6, slot(2), PG, PAD + NT)
        pool_a = part(W6, slot(2) + 2208, PAD + NT)
        pool_b = part(W6, slot(2) + 2760, PAD + NT)
        mix_sb = part(W6, slot(2) + 3312, PG, P)
        wi_sb = part(W6, slot(2) + 3824, KD, H)
        vexp = part(W6, slot(2) + 2208, 2, AW)
        pt = [part(W6, slot(2) + 512 * n, 512) for n in range(4)]
        causal0 = part(W6, slot(2) + 2048, P)
        strip = part(W6, slot(3), H, STRIP)
        score = part(W6, slot(3) + H * STRIP, SCORE_W)
        score_s = part(W6, slot(3) + H * STRIP + SCORE_W, KEYS_S)
        zi = part(W6, slot(3) + H * STRIP + SCORE_W + 1032, 320)
        lg = [part(W6, slot(5) + 528 * n, 528) for n in range(4)]
        mb = [part(W6, slot(2) + 3232, 528), part(W6, slot(5) + 2112, 528)]
        lg_s = part(W6, slot(5), 2, 257)
        ptz = part(W6, slot(5) + 514, 16, P)
        om = part(W6, slot(5) + 2562, 2, AW)
        bias_sb = part(W6, slot(3) + H * STRIP + SCORE_W + 1032, 256)
        kidx = part(HR, 0, 4, KEYS_S)
        relu_p = [part(X2, 528 * n, 528) for n in range(2)]
        relu_s = part(X2, 1056, KEYS_S)
        stT = part(X2, 2112, PG * NS, 15)
        zq = part(X2, 2592, 1040)
        sga = part(HR, 0, KD, NT)
        sbb = part(X2, 0, KD, NT)
        btmp = KI[:, :]
        qz = [qi_v[0], qT]
        wo = [part(W6, slot(n), KD, 512) for n in range(2)]

        def xn(t):
            return part(QK, D * t, D) if t < 4 else part(VN, 0, D)

        def hf(t):
            return part(X2, D * t, D) if t < 4 else part(VN, D, D)
        zrow = part(VN, 2 * D, 512)
        hfT = [part(QI, n * 1024, KD, P) for n in range(2)]
        gffn = part(WR, 0, D)
        gfin = part(WR, D, D)
        rt_log = part(WR, 2048, NTILE, NE)
        rt_eq = part(WR, 2208, NTILE, TOPE, NE)
        rt_eg = part(WR, 2848, NTILE, TOPE, NE)
        rt_m = part(WR, 3488, NTILE, NE)
        rt_g = part(WR, 3648, NTILE, NE)
        rt_e = part(WR, 3808, NTILE, 8)
        rt_w = part(WR, 3848, NTILE, TOPE)
        rt_br = part(WR, 3872, NE)
        rt_cnt = part(WR, 3904, NE)
        rt_before = part(XR, 0, NTILE + 1, NE)
        b_gu_sb = part(KI, 0, NE, 16)
        posv = part(X1, 4 * D, NTILE, SELS)
        gx = part(choices, 0, NTILE, SELS, 3)
        gT = part(X2, 700, NTILE, P)
        bd_sb = part(X2, 1340, D)
        xg = [part(X1, D * n, D) for n in range(2)]
        ysc = [part(X1, D * (2 + n), D) for n in range(2)]
        cmpm = [part(XR, NTILE * CAP * n, NTILE, CAP) for n in range(2)]
        hTe = part(XR, 960, KD, CAP)
        gu_t = [part(XR, 1728 + 384 * n, 4, CAP) for n in range(2)]
        sg_t = [part(XR, 2496 + 192 * n, 2, CAP) for n in range(2)]
        gs_t = part(XR, 2880, 2, CAP)
        act_t = part(XR, 3168, 2, CAP)
        yf = part(W6, 0, NTILE, D)
        junk = part(W6, slot(2), D)

        def small(at, n=1):
            return smalls[:, at:at + n]
        gmix_sb = small(0, 8)
        psc_sb = small(8, 4)
        wi_nat = small(12, 40).rearrange("p (t h) -> p t h", h=H)
        wcol = small(52)
        wblk = small(53, 8)
        max8 = small(61, 8)
        nmax = small(69, 40)
        esum = small(109, 40)
        rsum = small(149, 40)
        rms = small(189, 5)
        rms2 = small(194, 5)
        eps_t = small(200)
        sum4 = small(201, 5)
        gcol = [small(206 + n) for n in range(2)]
        spare = small(208)
        unused = [small(209 + n) for n in range(2)]
        iota_b = part(XR, 3072, CAP)
        top_v = part(WR, 3936, NTILE, 8)
        top_i = part(WR, 3976, NTILE, 8).bitcast(U32)

        PS = ctx.enter_context(nc.psum_tensor("PS", [P, 8, 512], F32))
        PSF = PS[:, :, :].rearrange("p a b -> p (a b)")

        def bank(n, w=512, at=0):
            return PSF[:, 512 * n + at:512 * n + at + w]
        PB = [PS[:, 0:2, :], PS[:, 2:4, :]]
        AB = [PSF[:, 4 * 512:6 * 512], PSF[:, 6 * 512:8 * 512]]
        SB_ = [PSF[:, 0:1024], PSF[:, 6 * 512:8 * 512]]
        PTB = [bank(2), bank(3)]
        L_g = [bank(4, 256), bank(5, 256)]
        L_n = [bank(6, 1)[0:32], bank(7, 1)[0:32]]
        O_g = [bank(5), bank(6)]
        AO = [bank(4), bank(5)]

        names = """Lqk_done acc_done acc_init act_ready act_taken all_added ao_taken as_ready attn_s_done b_mult
        bd_in bgu_in bias_in causal_done clamp_done cmp_ready cnt_ready cst_in log_taken w_high w_split part_used act_done act_high
        dots_ready dve_step dve_taken eps_set exp_done exps_done fin_gb fin_rs fin_sq fin_y gT_done
        gated gb_ready gmix_in gtr_ready gu_ready gu_taken hTe_ready h_done hfT_ready hfT_taken hf_done
        idx_ready kidx_in kinew_set kvu late_in lgp_done lgs_done m_done m_ready mask_done mb_done
        mb_ready mq_done mxT_ready nmax_s og_ready om_done ones_set out_done p_norm po_step pool_done
        pool_may pool_pad proj_done psT_ready ps_norm pt_ready pt_taken ptz_done pv_pair qz_done
        qi_zero qz_zero rank_ready relu_done router_ready row_ms s_ready sel_ready sidx_taken sig_done
        slot5_set slot_ready slots_moved small_in smask_done sq_done stT_in strip_in sums_ready
        unused_done up_done vnew_in vtail_out wblk_done wcol_in wi_out wo0_in wo1_in wv_in xn_in
        xt_ready y_ready zero_rows zi_set zq_done zq_zero ztmp_in""".split()
        S = {n: sem(n) for n in names}
        w_full = [sem(f"w_full{n}") for n in range(4)]
        kv_full = [sem(f"kv_full{n}") for n in range(2)]
        r_full = [sem(f"ring_full{n}") for n in range(6)]
        gath = [sem(f"gathered{n}") for n in range(2)]
        x_full = [sem(f"x_full{n}") for n in range(4)]
        yf_full = [sem(f"yf_full{n}") for n in range(NTILE)]
        scat = [sem(f"scattered{n}") for n in range(2)]

        J_SS, J_QI, J_KI, J_WI, J_K, J_Q, J_P, J_V, J_MIX, J_GATE = 0, 1, 5, 6, 7, 11, 15, 19, 24, 28
        zq_v = zq[:, 0:1032].rearrange("p (c x) -> p c x", x=258)
        J_A, J_WO = 52, 60
        N_MT = 17
        ITEMS = N_MT + 3 * KD + KD

        def job_of(n):
            if n < 5:
                return J_QI + n
            if n < N_MT:
                return J_K + n - 5
            return J_GATE + n - N_MT if n < N_MT + 3 * KD else J_A + n - N_MT - 3 * KD
        DOTS = [(t, h) for t in (4, 3, 2, 1) for h in range(H)]
        HEADS = [(t, h) for t in range(NTILE) for h in range(H)]

        def link(eng, ins, name, count):
            count[0] += 1
            ins.then_inc(S[name], 1)
            eng.wait_ge(S[name], count[0])

        block = ctx.enter_context(nc.Block())

        @block.sync
        def _(sp):
            def item(n):
                if n >= 4:
                    sp.wait_ge(S["proj_done"], job_of(n - 4) + 1)
                if n < N_MT:
                    src, w = w_mt[n], 1024
                elif n < N_MT + 3 * KD:
                    d, k = divmod(n - N_MT, 3)
                    src, w = ((w_mt[N_MT + 2 * d], 1024), (w_brp[d], 512), (w_mt[N_MT + 2 * d + 1], 1024))[k]
                else:
                    src, w = w_bra[n - N_MT - 3 * KD], 512
                sp.dma_start(wring[:, n % 4, 0:w], src).then_inc(w_full[n % 4], 16)

            def pages(n):
                if n >= 2:
                    sp.wait_ge(S["kvu"], n - 1)
                cache = cache_kT if n < NS else cache_v
                b = n % NS
                _, found = nc.values_load_multi_w_load_instructions(pt_sb[0:1, NPAGE * b:NPAGE * b + NPAGE], [SP], min_val=0, max_val=NPOOL - 1)
                for j, page in enumerate(found):
                    sp.dma_start(kv[n % 2][:, j, :], cache[bass.ds(page, 1)].rearrange("a p x -> (a p) x")).then_inc(kv_full[n % 2], 16)

            for k in range(4):
                sp.dma_start(x_in[:, 2 * k:2 * k + 2, :], xT[:, 2 * k:2 * k + 2, :]).then_inc(x_full[k], 16)
            sp.dma_start(cst[:, :], consts).then_inc(S["cst_in"], 16)
            sp.dma_start(gmix_sb, g_mix).then_inc(S["gmix_in"], 16)
            sp.dma_start(pt_sb[:, :], page_table).then_inc(S["small_in"], 16)
            sp.dma_start(psc_sb, pool_scale).then_inc(S["small_in"], 16)
            sp.dma_start(wi_sb, w_wi).then_inc(S["small_in"], 16)
            sp.dma_start(mix_sb, w_mix).then_inc(S["small_in"], 16)
            sp.dma_start(wr_sb[:, :, :], w_router).then_inc(S["small_in"], 16)
            sp.dma_start(bias_new, bias_n).then_inc(S["small_in"], 16)
            for n in range(4):
                item(n)
            sp.wait_ge(S["small_in"], 96)
            sp.wait_ge(S["h_done"], KD)
            sp.dma_start(stT, stateT).then_inc(S["stT_in"], 16)
            sp.dma_start(w_v_sb, w_v).then_inc(S["wv_in"], 16)
            for n in range(4, 9):
                item(n)
            sp.dma_start(strip, bias_strip).then_inc(S["strip_in"], 16)
            sp.wait_ge(S["dots_ready"], len(DOTS))
            sp.wait_ge(S["zi_set"], 16 * 16)
            sp.dma_start(o_state, state[:, 1:, :]).then_inc(S["out_done"], 16)
            for n in range(9, 12):
                item(n)
            pages(0)
            pages(1)
            for n in range(12, N_MT):
                item(n)
            sp.wait_ge(S["dots_ready"], len(DOTS) + 1)
            sp.dma_start(bias_sb, bias_s).then_inc(S["bias_in"], 16)
            for n in range(2, NS + 2):
                if n < 6:
                    item(N_MT + n - 2)
                pages(n)
            sp.wait_ge(S["act_taken"], J_V + NTILE)
            sp.dma_start(o_kT, kT).then_inc(S["out_done"], 16)
            sp.dma_start(o_kiT, kiT[0:64, :]).then_inc(S["out_done"], 16)
            sp.wait_ge(S["pool_done"], PG)
            sp.dma_start(o_v[0:4 * P].rearrange("(t p) x -> p t x", p=P), vN[:, 0:4, :]).then_inc(S["out_done"], 16)
            sp.dma_start(o_v[4 * P:NT], vN[0:TAIL, 4, :]).then_inc(S["vtail_out"], 16)
            sp.wait_ge(S["vtail_out"], 16)
            for b in range(NS):
                sp.dma_start(vexp[8 * (b % 4):8 * (b % 4) + 8, b // 4, :], o_v[NP_ + b].partition_broadcast(8)).then_inc(S["vnew_in"], 16)
            for d in range(KD):
                for k in range(3):
                    item(N_MT + 4 + 3 * d + k)
                    if 2 <= d < 5 and k != 1:
                        pages(NS + 2 * d - 2 + k // 2)

            def ring_load(c, e):
                if c < CHUNKS:
                    src = w_gu[bass.ds(e, 1), c].rearrange("a p x -> (a p) x")
                else:
                    src = w_down[bass.ds(e, 1), c - CHUNKS].rearrange("a p x -> (a p) x")
                sp.dma_start(W6[:, slot(c):slot(c + 1)], src).then_inc(r_full[c], 16)

            sp.wait_ge(S["kvu"], 2 * NS)
            sp.dma_start(wo[0], w_out[0]).then_inc(S["wo0_in"], 16)
            sp.dma_start(wo[1], w_out[1]).then_inc(S["wo1_in"], 16)
            sp.wait_ge(S["ao_taken"], NTILE)
            for n in range(N_MT + 4 + 3 * KD, ITEMS):
                item(n)
            for t in range(NTILE):
                sp.dma_start(xn(t)[0:TROWS[t]], xnat[t * P:t * P + TROWS[t]]).then_inc(S["xn_in"], 16)
            for c in range(2, 6):
                ring_load(c, 0)
            sp.dma_start(b_gu_sb, b_gu).then_inc(S["bgu_in"], 16)
            sp.wait_ge(S["proj_done"], J_A + KD)
            sp.dma_start(gffn, g_ffn.partition_broadcast(P)).then_inc(S["late_in"], 16)
            sp.dma_start(gfin, g_final.partition_broadcast(P)).then_inc(S["late_in"], 16)
            sp.dma_start(rt_br, b_router.partition_broadcast(P)).then_inc(S["late_in"], 16)
            for t in range(NTILE):
                sp.wait_ge(S["dve_taken"], KD + t + 1)
                sp.dma_start(y_acc[t * P:t * P + TROWS[t]], xn(t)[0:TROWS[t]]).then_inc(S["acc_init"], 16)
                sp.wait_ge(S["hf_done"], t + 1)
                sp.dma_start(h_rows[t * P:t * P + TROWS[t]], hf(t)[0:TROWS[t]]).then_inc(S["acc_init"], 16)
            for c in range(2):
                ring_load(c, 0)
            sp.wait_ge(S["acc_init"], 16 * 2 * NTILE)
            sp.wait_ge(S["hfT_ready"], NTILE)
            sp.dma_start(bd_sb[0:NE], b_down).then_inc(S["bd_in"], 16)

            def experts(b, first):
                with sp.Fori(first, NE) as e:
                    for c in range(CHUNKS):
                        sp.wait_ge(S["gu_ready"], (b * NE + e - 1) * CHUNKS + c + 1)
                        ring_load(c, e)
                    for c in range(2):
                        sp.wait_ge(S["w_split"], (b * NE + e - 1) * KD + 4 * c + 4)
                        ring_load(CHUNKS + c, e)
            experts(0, 1)
            sp.wait_ge(S["cnt_ready"], 1)
            most = sp.value_load(cnt_i[0:1, 0:1], min_val=0, max_val=NT)
            with sp.Fori(1, PASSES) as b:
                with sp.If(b * CAP < most):
                    experts(b, 0)
            sp.wait_ge(S["all_added"], 1)
            for t in range(NTILE):
                sp.dma_start(yf[0:TROWS[t], t, :], y_acc[t * P:t * P + TROWS[t]]).then_inc(yf_full[t], 16)
            for t in range(NTILE):
                sp.wait_ge(S["fin_y"], t + 1)
                sp.dma_start(o_y[t * P:t * P + TROWS[t]], yf[0:TROWS[t], t, :]).then_inc(S["out_done"], 16)
            sp.wait_ge(S["out_done"], 16 * (4 + NTILE))

        @block.gpsimd
        def _(po):
            n = [0]
            po.wait_ge(S["cst_in"], 16)
            po.memset(ones[:, :], 1.0).then_inc(S["ones_set"], 1)
            po.memset(eps_t, EPS).then_inc(S["eps_set"], 1)
            po.wait_ge(S["ones_set"], 1)
            po.wait_ge(S["eps_set"], 1)
            link(po, po.memset(zi, 0.0), "po_step", n)
            po.wait_ge(S["small_in"], 96)
            for b in range(NS):
                _, found = nc.values_load_multi_w_load_instructions(pt_sb[0:1, NPAGE * b:NPAGE * b + NPAGE], [POOL], min_val=0, max_val=NPOOL - 1)
                for g, page in enumerate(found):
                    lo = 64 * (b % 2)
                    po.dma_start(kidx[lo:lo + 64, b // 2, g * PAGE:g * PAGE + PAGE], cache_kiT[bass.ds(page, 1)].rearrange("a p x -> (a p) x"))\
                        .then_inc(S["kidx_in"], 16)
            po.wait_ge(S["act_taken"], J_QI + 4)
            ziv = zi.rearrange("p (j x) -> p j x", x=80)
            for r in range(2):
                for hp in range(2):
                    for j in range(4):
                        po.dma_start(ziv[64 * r:64 * r + 64, j, 8 * r + hp:8 * r + hp + 8:2],
                                     qi_v[hp][64 * hp:64 * hp + 64, :, NP_ + r + 2 * j], allow_slow_non_contiguous=True).then_inc(S["zi_set"], 16)
            po.wait_ge(S["act_taken"], J_KI + 1)
            for r in range(2):
                po.tensor_copy(kidx[64 * r:64 * r + 64, :, PAST], kiT[64 * r:64 * r + 64, NP_ + r:NT:2]).then_inc(S["kinew_set"], 1)
                po.wait_ge(S["kinew_set"], r + 1)
            po.wait_ge(S["act_taken"], J_WI + 1)
            po.dma_start(wi_row, wi_nat[META:META + NS, 4, :]).then_inc(S["wi_out"], 16)
            po.wait_ge(S["wi_out"], 16)
            po.dma_start(wcol[0:64], wi_row.rearrange("b (h o) -> (b h) o", o=1)).then_inc(S["wcol_in"], 16)
            po.wait_ge(S["wcol_in"], 16)
            po.tensor_scalar(wblk[0:64], wsel, wcol[0:64], None, ALU.mult).then_inc(S["wblk_done"], 1)
            po.wait_ge(S["sq_done"], KD)
            po.wait_ge(S["h_done"], KD)
            po.memset(zq, 0.0).then_inc(S["zq_zero"], 1)
            po.wait_ge(S["zq_zero"], 1)
            po.wait_ge(S["wblk_done"], 1)
            for i, t in enumerate((4, 3, 2, 1)):
                po.wait_ge(S["acc_done"], H * (i + 1))
                v = score[0:ROWS[t], SCORE_AT[t] + P * t:SCORE_AT[t] + KEYS[t]]
                po.affine_select(out=v, in_=v, compare_op=ALU.is_ge, fill=NONCAUSAL, base=0,
                                 pattern=[[-1, ROWS[t]]], channel_multiplier=1).then_inc(S["causal_done"], 1)
                po.wait_ge(S["causal_done"], i + 1)
            po.wait_ge(S["pool_pad"], 1)
            po.wait_ge(S["stT_in"], 16)
            for g in range(PG):
                w = 2 << g
                po.wait_ge(S["act_taken"], J_P + g + 1)
                src = pT[:, g, :]
                for s in range(g + 1):
                    dst = pool_a if s % 2 == 0 else pool_b
                    link(po, po.tensor_tensor(dst[:, PAD:PAD + NP_], src[:, PAD:PAD + NP_],
                                              src[:, PAD - (1 << s):PAD + NP_ - (1 << s)], ALU.add), "po_step", n)
                    src = dst
                sd = src[:, PAD + NP_:PAD + NT]
                st = stT[:, NS * g:NS * g + NS, :]
                link(po, po.tensor_tensor(sd, pT[:, g, PAD + NP_:PAD + NT], st[:, :, 14], ALU.add), "po_step", n)
                for k in range(2, w):
                    link(po, po.tensor_tensor(sd, sd, st[:, :, 15 - k], ALU.add), "po_step", n)
                link(po, po.tensor_tensor(src[:, PAD:2 * PAD], src[:, PAD:2 * PAD], rcnt[:, g, :], ALU.mult), "po_step", n)
                link(po, po.tensor_scalar(src[:, 2 * PAD:], src[:, 2 * PAD:], 1.0 / w, None, ALU.mult), "po_step", n)
                po.dma_start(o_pT[:, g, :], pT[:, g, PAD + NP_ - 15:PAD + NT]).then_inc(S["ztmp_in"], 16)
                po.wait_ge(S["ztmp_in"], 16 * (g + 1))
                po.tensor_tensor(pT[:, g, PAD:], src[:, PAD:], pT[:, g, PAD:], ALU.subtract).then_inc(S["pool_done"], 1)
                po.wait_ge(S["pool_done"], g + 1)
            po.wait_ge(S["act_taken"], J_V + NTILE)
            link(po, po.memset(ptz, 0.0), "po_step", n)
            po.memset(lg_s[:, :, 256:257], OUT).then_inc(S["slot5_set"], 1)
            po.wait_ge(S["slot5_set"], 1)
            po.wait_ge(S["zq_done"], 4)
            po.wait_ge(S["qz_done"], 1)
            po.memset(qT[0:64], 0.0).then_inc(S["qz_zero"], 1)
            po.wait_ge(S["qz_zero"], 1)
            for d in range(KD):
                po.wait_ge(S["act_taken"], J_GATE + 3 * d + 2)
                po.tensor_tensor(sbb[:, d, :], sbb[:, d, :], btmp, ALU.mult).then_inc(S["b_mult"], 1)
                po.wait_ge(S["b_mult"], d + 1)
            po.wait_ge(S["act_taken"], J_A)
            link(po, po.memset(causal0, 0.0), "po_step", n)
            link(po, po.affine_select(out=causal0, in_=causal0, compare_op=ALU.is_ge, fill=OUT, base=0,
                                      pattern=[[-1, P]], channel_multiplier=1), "po_step", n)
            po.wait_ge(S["strip_in"], 16)
            for i, (t, h) in enumerate(HEADS):
                if i == 1:
                    po.wait_ge(S["attn_s_done"], 2)
                if h == 0 and t:
                    po.wait_ge(S["mask_done"], t)
                if i >= 2:
                    po.wait_ge(S["lgp_done"], i - 1)
                r, w = ROWS[t], KEYS[t]
                m = causal0 if t == 0 else score[:, SCORE_AT[t]:SCORE_AT[t] + w]
                po.tensor_tensor(mb[i % 2][0:r, 0:w], m[0:r], strip[0:r, h, 512 - P * t:512 - P * t + w], ALU.add)\
                    .then_inc(S["mb_done"], 1)
                po.wait_ge(S["mb_done"], i + 1)
            po.wait_ge(S["m_done"], KD)
            link(po, po.memset(zrow[0:CAP], 0.0), "po_step", n)
            for a in range(2):
                po.dma_start(y_acc[NT:NT + CAP, 512 * a:512 * a + 512], zrow[0:CAP]).then_inc(scat[a], 16)
                po.wait_ge(scat[a], 16)
                po.dma_start(h_rows[NT:NT + CAP, 512 * a:512 * a + 512], zrow[0:CAP]).then_inc(S["zero_rows"], 16)
            po.wait_ge(S["zero_rows"], 32)
            po.wait_ge(S["acc_init"], 16 * 2 * NTILE)

            def gather(b, e, u):
                po.wait_ge(S["idx_ready"], b * SELS + e + 1)
                po.sem_inc(S["pool_may"], 1)
                po.indirect_dma_start(xg[u][0:CAP], None, h_rows, bass.IndirectOffsetOnAxis(ap=idx_i[u][0:CAP, :], axis=0))\
                    .then_inc(gath[u], 16)

            def experts(b):
                gather(b, 0, 0)
                with po.Fori(0, NE // 2) as i:
                    for u in range(2):
                        e = i * 2 + u
                        gather(b, e + 1, 1 - u)
                        if u == 0:
                            po.wait_ge(scat[1], (b * (NE // 2) + i + 1) * 16)
                        else:
                            po.wait_ge(scat[0], (b * (NE // 2) + i + 2) * 16)
                        po.wait_ge(S["y_ready"], b * NE + e + 2)
                        po.sem_inc(S["pool_may"], 1)
                        po.indirect_dma_start(y_acc, bass.IndirectOffsetOnAxis(ap=idx_i[u][0:CAP, :], axis=0),
                                              ysc[u][0:CAP], None, compute_op=ALU.add).then_inc(scat[u], 16)
                po.wait_ge(scat[1], (b * (NE // 2) + NE // 2 + 1) * 16)

            po.wait_ge(S["cnt_ready"], 1)
            most = po.value_load(cnt_i[0:1, 0:1], min_val=0, max_val=NT)
            experts(0)
            with po.Fori(1, PASSES) as b:
                with po.If(b * CAP < most):
                    experts(b)
            po.wait_ge(S["cnt_ready"], 1)
            po.memset(spare, 0.0).then_inc(S["all_added"], 1)

        @block.scalar
        def _(act):
            def take(j, dst, src, func=ACT.Copy, scale=1.0):
                act.wait_ge(S["proj_done"], j + 1)
                return nc.scalar.activation(dst, src, func, scale=scale)

            def wide(j):
                return PB[j % 2][:, :, 0:HALF]

            def halves(ap):
                return ap.rearrange("p (a b) -> p a b", a=2)

            for k in range(KD):
                if k % 2 == 0:
                    act.wait_ge(x_full[k // 2], 16)
                act.activation(sq[:, k, :], x_in[:, k, :], ACT.Square).then_inc(S["sq_done"], 1)
            act.wait_ge(S["eps_set"], 1)
            act.wait_ge(S["proj_done"], 1)
            nc.scalar.activation(halves(KI[:, :]), wide(0), ACT.Sqrt, bias=eps_t, scale=1.0 / D).then_inc(S["act_taken"], 1)
            for c in range(4):
                take(J_QI + c, halves(qi_v[0][0:64, c, :]), wide(J_QI + c)[0:64])
                take(J_QI + c, halves(qi_v[1][64:128, c, :]), wide(J_QI + c)[64:128]).then_inc(S["act_taken"], 1)
            act.wait_ge(S["h_done"], KD)
            take(J_KI, halves(kiT), wide(J_KI)).then_inc(S["act_taken"], 1)
            act.wait_ge(S["proj_done"], J_WI + 1)
            nc.scalar.activation(wi_nat[:, 0:4, :], PB[J_WI % 2][:, 0, 0:32].rearrange("p (t h) -> p t h", h=H), ACT.Copy)
            nc.scalar.activation(wi_nat[0:TAIL, 4, :], PB[J_WI % 2][0:TAIL, 0, 32:40], ACT.Copy).then_inc(S["act_taken"], 1)
            for i, (t, h) in enumerate(DOTS):
                act.wait_ge(S["dots_ready"], i + 1)
                if i >= 2:
                    act.wait_ge(S["acc_done"], i - 1)
                act.activation(relu_p[i % 2][0:ROWS[t], 0:KEYS[t]], AB[i % 2][0:ROWS[t], 0:KEYS[t]], ACT.Relu)\
                    .then_inc(S["relu_done"], 1)
            for c in range(4):
                take(J_K + c, halves(kT[:, c, :]), wide(J_K + c)).then_inc(S["act_taken"], 1)
            act.wait_ge(S["dots_ready"], len(DOTS) + 1)
            act.activation(relu_s[0:64], PSF[0:64, 4 * 512:4 * 512 + KEYS_S], ACT.Relu).then_inc(S["relu_done"], 1)
            for c in range(4):
                take(J_Q + c, halves(qT[:, c, :]), wide(J_Q + c), scale=HD ** -0.5).then_inc(S["act_taken"], 1)
            act.wait_ge(S["act_taken"], J_Q + 4)
            act.wait_ge(S["zq_zero"], 1)
            for hp in range(2):
                for g in range(2):
                    act.activation(zq_v[64 * hp:64 * hp + 64, :, 128 * g + hp:128 * g + hp + 121:40],
                                   qT[64 * hp:64 * hp + 64, :, NP_ + 4 * g:NP_ + 4 * g + 4], ACT.Copy).then_inc(S["zq_done"], 1)
            act.wait_ge(S["dots_ready"], len(DOTS))
            act.wait_ge(S["zi_set"], 16 * 16)
            act.activation(qz[0][0:64], qT[0:64], ACT.Copy).then_inc(S["qz_done"], 1)
            act.wait_ge(S["pool_pad"], 1)
            for g in range(PG):
                take(J_P + g, halves(pT[:, g, PAD:]), wide(J_P + g)).then_inc(S["act_taken"], 1)
            for t in range(NTILE):
                r = TROWS[t]
                take(J_V + t, vN[0:r, t, :], PB[(J_V + t) % 2][0:r, 0, :]).then_inc(S["act_taken"], 1)
            for g in range(PG):
                act.wait_ge(S["small_in"], 96)
                take(J_MIX + g, halves(pT[:, g, PAD:]), wide(J_MIX + g), scale=psc_sb[:, g:g + 1]).then_inc(S["act_taken"], 1)
            act.wait_ge(S["acc_done"], len(DOTS))
            act.wait_ge(S["sidx_taken"], 1)
            act.wait_ge(S["pool_done"], PG)
            for d in range(KD):
                j = J_GATE + 3 * d
                take(j, halves(sbb[:, d, :]), wide(j), ACT.Sigmoid).then_inc(S["act_taken"], 1)
                if d == 0:
                    act.wait_ge(S["out_done"], 16 * 4)
                else:
                    act.wait_ge(S["b_mult"], d)
                act.wait_ge(S["proj_done"], j + 2)
                nc.scalar.activation(halves(btmp), wide(j + 1), ACT.Copy).then_inc(S["act_taken"], 1)
                take(j + 2, halves(sga[:, d, :]), wide(j + 2), ACT.Sigmoid).then_inc(S["act_taken"], 1)
                if d == 0:
                    act.wait_ge(S["nmax_s"], 1)
                    for g in range(2):
                        act.activation(lg_s[:, g, :], lg_s[:, g, :], ACT.Exp, bias=nmx2[:, g:g + 1], accum_out=es2[:, g:g + 1])\
                            .then_inc(S["exps_done"], 1)

            def pt_out(i):
                t = HEADS[i][0]
                act.wait_ge(S["pt_ready"], i + 1)
                if i >= 4:
                    act.wait_ge(S["pv_pair"], i // 2 - 1)
                r, nk = ROWS[t], -(-KEYS[t] // P)
                if t < 4:
                    act.activation(pt[i % 4][:, 0:nk * r], PTB[i % 2][:, 0:nk * r], ACT.Copy).then_inc(S["pt_taken"], 1)
                else:
                    act.activation(pt[i % 4][:, 0:4 * r], PTB[i % 2][:, 0:4 * r], ACT.Copy)
                    act.activation(pt[i % 4][0:META, 4 * r:5 * r], PTB[i % 2][0:META, 4 * r:5 * r], ACT.Copy).then_inc(S["pt_taken"], 1)

            def ao_out(t):
                act.wait_ge(S["pv_pair"], 4 * t + 4)
                r = ROWS[t]
                act.activation(attnT[:, :, P * t:P * t + r], AO[t % 2][:, 0:4 * r].rearrange("p (c r) -> p c r", c=4), ACT.Copy)\
                    .then_inc(S["ao_taken"], 1)

            for i, (t, h) in enumerate(HEADS):
                r, w = ROWS[t], KEYS[t]
                act.wait_ge(S["lgp_done"], i + 1)
                act.activation(lg[i % 4][0:r, 0:w], lg[i % 4][0:r, 0:w], ACT.Exp, bias=nmax[0:r, i:i + 1], scale=-1.0,
                               accum_out=esum[0:r, i:i + 1]).then_inc(S["exp_done"], 1)
                if i >= 2:
                    pt_out(i - 2)
                if h == 3 and t:
                    ao_out(t - 1)
            pt_out(len(HEADS) - 2)
            pt_out(len(HEADS) - 1)
            ao_out(NTILE - 1)

            def hfT_out(t):
                r = TROWS[t]
                act.wait_ge(S["hfT_ready"], t + 1)
                if t >= 2:
                    act.wait_ge(S["router_ready"], t - 1)
                act.activation(hfT[t % 2][:, :, 0:r], PSF[:, 3072:3072 + KD * r].rearrange("p (k r) -> p k r", k=KD),
                               ACT.Copy).then_inc(S["hfT_taken"], 1)
            for t in range(NTILE):
                r = TROWS[t]
                act.wait_ge(S["dve_taken"], KD + t + 1)
                act.wait_ge(S["m_done"], KD)
                act.activation(hf(t)[0:r], xn(t)[0:r], ACT.Square, accum_out=rms[0:r, t:t + 1]).then_inc(S["row_ms"], 1)
                act.wait_ge(S["row_ms"], 2 * t + 1)
                act.activation(rms[0:r, t:t + 1], rms[0:r, t:t + 1], ACT.Sqrt, bias=eps_t[0:r], scale=1.0 / D).then_inc(S["row_ms"], 1)
                if t:
                    hfT_out(t - 1)
            hfT_out(NTILE - 1)

            act.wait_ge(S["sel_ready"], 1)
            act.activation(rt_w, rt_w, ACT.Exp).then_inc(S["sel_ready"], 1)

            def hTe_out(n):
                act.wait_ge(S["xt_ready"], n)
                act.activation(hTe.rearrange("p (a k) s -> p a (k s)", a=2), PS[:, 2:4, 0:4 * CAP], ACT.Copy).then_inc(S["hTe_ready"], 1)

            def high(ne, f):
                act.wait_ge(r_full[CHUNKS + f // 4], (ne + 1) * 16)
                act.wait_ge(S["part_used"], ne * KD + f + 1)
                act.activation(w_hi[:, f % 4, :], W6[:, slot(4) + D * f:slot(4) + D * f + D], ACT.Copy).then_inc(S["w_high"], 1)

            def experts(b):
                hTe_out(b * SELS + 1)
                with act.Fori(0, NE // 2) as i:
                    for u in range(2):
                        e = i * 2 + u
                        for c in range(CHUNKS):
                            act.wait_ge(S["clamp_done"], (b * NE + e) * CHUNKS + c + 1)
                            act.activation(sg_t[c % 2], gu_t[c % 2][:, 0:2, :], ACT.Sigmoid, scale=1.702).then_inc(S["sig_done"], 1)
                            high(b * NE + e, c)
                        hTe_out(b * SELS + e + 2)
                        for f in range(CHUNKS, KD):
                            high(b * NE + e, f)
                        act.wait_ge(scat[u], (b * (NE // 2) + i + 1) * 16)
                        act.wait_ge(S["part_used"], (b * NE + e + 1) * KD + 4)
                        act.activation(ysc[u][0:CAP], PSF[0:CAP, 4 * 512:6 * 512], ACT.Copy, scale=gcol[u][0:CAP]).then_inc(S["y_ready"], 1)
            act.wait_ge(S["cnt_ready"], 1)
            act.sem_inc(S["y_ready"], 1)
            most = act.value_load(cnt_i[0:1, 0:1], min_val=0, max_val=NT)
            experts(0)
            with act.Fori(1, PASSES) as b:
                with act.If(b * CAP < most):
                    experts(b)
            for t in range(NTILE):
                r = TROWS[t]
                act.wait_ge(S["fin_gb"], t + 1)
                act.activation(junk[0:r], yf[0:r, t, :], ACT.Square, accum_out=rms2[0:r, t:t + 1]).then_inc(S["fin_sq"], 1)
                act.wait_ge(S["fin_sq"], t + 1)
                act.activation(rms2[0:r, t:t + 1], rms2[0:r, t:t + 1], ACT.Sqrt, bias=eps_t[0:r], scale=1.0 / D).then_inc(S["fin_rs"], 1)

        @block.tensor
        def _(pe):
            used = [0]

            def free(j):
                if j < 2:
                    return
                if j - 2 < J_A:
                    pe.wait_ge(S["act_taken"], j - 1)
                else:
                    pe.wait_ge(S["dve_taken"], j - 1 - J_A)

            def project(j, lhs, rhs, nk, item=True, rows=P):
                free(j)
                if item:
                    n = used[0]
                    pe.wait_ge(w_full[n % 4], 16 * (n // 4 + 1))
                for a in range(2):
                    for k in range(nk):
                        mm = pe.matmul(PB[j % 2][0:rows, a, 0:HALF], lhs(k), rhs(k)[:, HALF * a:HALF * a + HALF],
                                       start=(k == 0), stop=(k == nk - 1))
                mm.then_inc(S["proj_done"], 1)
                used[0] += item

            def w(k):
                return wring[:, used[0] % 4, P * k:P * k + P]

            def hk(k):
                return hT[:, k, :]

            pe.wait_ge(S["ones_set"], 1)
            pe.wait_ge(S["cst_in"], 16)
            for a in range(2):
                for k in range(KD):
                    if a == 0:
                        pe.wait_ge(S["sq_done"], k + 1)
                    mm = pe.matmul(PB[0][:, a, 0:HALF], ones[:, :], sq[:, k, HALF * a:HALF * a + HALF], start=(k == 0), stop=(k == KD - 1))
            mm.then_inc(S["proj_done"], 1)
            pe.wait_ge(w_full[0], 16)
            for k in range(KD):
                pe.wait_ge(S["h_done"], k + 1)
                for a in range(2):
                    mm = pe.matmul(PB[J_QI % 2][:, a, 0:HALF], w(k), hk(k)[:, HALF * a:HALF * a + HALF], start=(k == 0), stop=(k == KD - 1))
            mm.then_inc(S["proj_done"], 1)
            used[0] = 1
            for c in range(1, 4):
                project(J_QI + c, w, hk, KD)
            project(J_KI, w, hk, KD)
            free(J_WI)
            pe.wait_ge(S["small_in"], 96)
            for t in range(NTILE):
                for k in range(KD):
                    mm = pe.matmul(PB[J_WI % 2][0:TROWS[t], 0, H * t:H * t + H], hT[:, k, P * t:P * t + TROWS[t]], wi_sb[:, k, :],
                                   start=(k == 0), stop=(k == KD - 1))
            mm.then_inc(S["proj_done"], 1)
            pe.wait_ge(S["act_taken"], J_KI + 1)
            pe.wait_ge(S["qi_zero"], 2)
            for i, (t, h) in enumerate(DOTS):
                if i >= 2:
                    pe.wait_ge(S["relu_done"], i - 1)
                for a in range(0, KEYS[t], 512):
                    z = min(KEYS[t], a + 512)
                    mm = pe.matmul(AB[i % 2][0:ROWS[t], a:z], qi_v[h % 2][:, h // 2, P * t:P * t + ROWS[t]], kiT[:, a:z],
                                   start=True, stop=True)
                mm.then_inc(S["dots_ready"], 1)
            for c in range(4):
                project(J_K + c, w, hk, KD)
            pe.wait_ge(S["relu_done"], len(DOTS))
            pe.wait_ge(S["zi_set"], 16 * 16)
            pe.wait_ge(S["kinew_set"], 2)
            pe.wait_ge(S["kidx_in"], 16 * NS * NPAGE)
            for a in range(3):
                lo, hi = 512 * a, min(KEYS_S, 512 * a + 512)
                for j in range(4):
                    mm = pe.matmul(PSF[0:64, 4 * 512 + lo:4 * 512 + hi], zi[:, 64 * j:64 * j + 64], kidx[:, j, lo:hi],
                                   start=(j == 0), stop=(j == 3))
            mm.then_inc(S["dots_ready"], 1)
            project(J_Q, w, hk, KD)
            pe.wait_ge(S["relu_done"], len(DOTS) + 1)
            pe.wait_ge(S["wblk_done"], 1)
            for a in range(3):
                lo, hi = 512 * a, min(KEYS_S, 512 * a + 512)
                mm = pe.matmul(PSF[0:NS, 4 * 512 + lo:4 * 512 + hi], wblk[0:64], relu_s[0:64, lo:hi], start=True, stop=True)
            mm.then_inc(S["dots_ready"], 1)
            for c in range(1, 4):
                project(J_Q + c, w, hk, KD)

            def qk_sample(b):
                g, m = divmod(b, 4)
                if b == 0:
                    pe.wait_ge(S["zq_done"], 4)
                    pe.wait_ge(S["sidx_taken"], 1)
                pe.wait_ge(kv_full[b % 2], 128 * (b // 2 + 1))
                for c in range(4):
                    block = zq[:, 256 * c + 32 * b:256 * c + 32 * b + 32]
                    for j in range(4):
                        mm = pe.matmul(L_g[g][32 * j:32 * j + 32], block, kv[b % 2][:, 2 * j:2 * j + 2, P * c:P * c + P],
                                       start=(m == 0 and c == 0), stop=False, skip_group_check=True)
                    if c == 3:
                        mm.then_inc(S["kvu"], 1)
                    pe.matmul(L_n[g], block, kT[:, c, NP_ + b:NP_ + b + 1], start=(m == 0 and c == 0), stop=False, skip_group_check=True)

            for g in range(PG):
                project(J_P + g, w, hk, KD)
                qk_sample(g)
            pe.wait_ge(S["wv_in"], 16)
            for t in range(NTILE):
                free(J_V + t)
                for k in range(KD):
                    mm = pe.matmul(PB[(J_V + t) % 2][0:TROWS[t], 0, :], hT[:, k, P * t:P * t + TROWS[t]], w_v_sb[:, k, :],
                                   start=(k == 0), stop=(k == KD - 1))
                mm.then_inc(S["proj_done"], 1)
                if PG + t < NS:
                    qk_sample(PG + t)
            for g in range(PG):
                pe.wait_ge(S["pool_done"], g + 1)
                project(J_MIX + g, lambda k: mix_sb[:, g, :], lambda k: pT[:, g, PAD:], 1, item=False)
            pe.wait_ge(S["smask_done"], 1)
            for g in range(2):
                for j in range(4):
                    pe.matmul(L_g[g][32 * j:32 * j + 32], selg[:, g, :], score_s[0:NS, 256 * j:256 * j + 256], start=False, stop=True,
                              skip_group_check=True)
                mm = pe.matmul(L_n[g], selg[:, g, :], score_s[0:NS, PAST:KEYS_S], start=False, stop=True, skip_group_check=True)
            mm.then_inc(S["Lqk_done"], 1)

            def sample_max():
                pe.wait_ge(S["lgs_done"], 1)
                pe.transpose(bank(7, P)[0:2], mx2, ident).then_inc(S["mxT_ready"], 1)

            def sample_max_back():
                pe.wait_ge(S["mq_done"], 1)
                pe.transpose(bank(7, 2, P), mq4, ident[0:2, 0:2]).then_inc(S["mb_ready"], 1)

            def sample_sums():
                pe.wait_ge(S["exps_done"], 2)
                pe.matmul(bank(7, 2, 132), same32, es2, start=True, stop=True).then_inc(S["sums_ready"], 1)

            def sample_turn():
                pe.wait_ge(S["ps_norm"], 2)
                for g in range(2):
                    for u in range(2):
                        mm = pe.transpose(bank(7, P, P * (2 * g + u)), lg_s[:, g, P * u:P * u + P], ident)
                mm.then_inc(S["psT_ready"], 1)

            def pv_sample(b):
                g, m = divmod(b, 4)
                n = NS + b
                pe.wait_ge(kv_full[n % 2], 128 * (n // 2 + 1))
                if b == 0:
                    pe.wait_ge(S["ptz_done"], 2)
                for u in range(2):
                    for j in range(4):
                        mm = pe.matmul(O_g[g][32 * j:32 * j + 32], ptz[:, 4 * (2 * g + u) + j, 32 * m:32 * m + 32], kv[n % 2][:, 2 * j + u, :],
                                       start=(m == 0 and u == 0), stop=(m == 3 and u == 1 and j > 0), skip_group_check=True)
                mm.then_inc(S["kvu"], 1)
                if m == 3:
                    pe.wait_ge(S["vnew_in"], 16 * NS)
                    pe.matmul(O_g[g][0:32], dnew[:, g, :], vexp[0:32, g, :], start=False, stop=True, skip_group_check=True)\
                        .then_inc(S["og_ready"], 1)

            def sample_out(g):
                pe.wait_ge(S["om_done"], g + 1)
                for c in range(4):
                    mm = pe.matmul(bank(7 - 3 * g, 4, 4 * c), om[:, g, P * c:P * c + P], selm, start=True, stop=True)
                mm.then_inc(S["as_ready"], 1)

            pm = lambda k: pT[:, k, PAD:]
            for d in range(KD):
                j = J_GATE + 3 * d
                project(j, w, hk, KD)
                if 2 <= d < 6:
                    pv_sample(2 * d - 4)
                if d == 0:
                    sample_max()
                    pe.wait_ge(S["act_taken"], J_MIX + PG)
                if d == 1:
                    sample_sums()
                project(j + 1, w, pm, PG)
                if d == 0:
                    sample_max_back()
                project(j + 2, w, hk, KD)
                if d == 1:
                    sample_turn()
                if 2 <= d < 6:
                    pv_sample(2 * d - 3)
                if d >= 6:
                    sample_out(d - 6)

            def logits(i):
                t, h = HEADS[i]
                if i >= 2:
                    pe.wait_ge(S["lgp_done"], i - 1)
                for a in range(0, KEYS[t], 512):
                    z = min(KEYS[t], a + 512)
                    mm = pe.matmul(SB_[i % 2][0:ROWS[t], a:z], qz[h % 2][:, h // 2, P * t:P * t + ROWS[t]], kT[:, h // 2, a:z],
                                   start=True, stop=True)
                mm.then_inc(S["s_ready"], 1)

            def turn(i):
                t, h = HEADS[i]
                r = ROWS[t]
                pe.wait_ge(S["p_norm"], i + 1)
                if i >= 2:
                    pe.wait_ge(S["pt_taken"], i - 1)
                for a in range(0, KEYS[t], P):
                    z = min(KEYS[t], a + P)
                    mm = pe.transpose(PTB[i % 2][0:z - a, a // P * r:a // P * r + r], lg[i % 4][0:r, a:z], ident[0:r, 0:r])
                mm.then_inc(S["pt_ready"], 1)

            def values(c, t):
                i = H * t + 2 * c
                r = ROWS[t]
                pe.wait_ge(S["pt_taken"], i + 2)
                if c == 0 and t >= 2:
                    pe.wait_ge(S["ao_taken"], t - 1)
                for a in range(0, KEYS[t], P):
                    z = min(KEYS[t], a + P)
                    for hp in range(2):
                        mm = pe.matmul(AO[t % 2][64 * hp:64 * hp + 64, c * r:c * r + r], vN[0:z - a, a // P, P * c + HD * hp:P * c + HD * hp + HD],
                                       pt[(i + hp) % 4][0:z - a, a // P * r:a // P * r + r], start=(a == 0), stop=(z == KEYS[t]))
                mm.then_inc(S["pv_pair"], 1)

            pe.wait_ge(S["act_taken"], J_A)
            pe.wait_ge(S["qz_done"], 1)
            pe.wait_ge(S["qz_zero"], 1)
            logits(0)
            pe.wait_ge(S["attn_s_done"], 2)
            for i in range(1, len(HEADS) + 3):
                if i < len(HEADS):
                    logits(i)
                if 2 <= i < len(HEADS) + 2:
                    turn(i - 2)
                if i >= 4 and i % 2 == 0:
                    values((i - 4) % H // 2, (i - 4) // H)

            pe.wait_ge(S["ao_taken"], NTILE)
            pe.wait_ge(S["lgp_done"], len(HEADS))
            pe.wait_ge(S["pt_taken"], len(HEADS))
            for d in range(KD):
                project(J_A + d, w, lambda k: attnT[:, k, :], 4)
            pe.wait_ge(S["m_done"], KD)
            pe.wait_ge(S["wo0_in"], 16)
            pe.wait_ge(S["wo1_in"], 16)

            def hf_turn(t):
                r = TROWS[t]
                if t:
                    pe.wait_ge(S["hfT_taken"], t)
                pe.wait_ge(S["hf_done"], t + 1)
                for k in range(KD):
                    mm = pe.transpose(PSF[:, 3072 + r * k:3072 + r * k + r], hf(t)[0:r, P * k:P * k + P], ident[0:r, 0:r])
                mm.then_inc(S["hfT_ready"], 1)

            def route(t):
                r = TROWS[t]
                pe.wait_ge(S["hfT_taken"], t + 1)
                if t >= 2:
                    pe.wait_ge(S["log_taken"], t - 1)
                for k in range(KD):
                    mm = pe.matmul(bank(4 + t % 2, NE)[0:r], hfT[t % 2][:, k, 0:r], wr_sb[:, k, :], start=(k == 0), stop=(k == KD - 1))
                mm.then_inc(S["router_ready"], 1)

            for t in range(NTILE):
                j, r = J_WO + t, TROWS[t]
                free(j)
                for a in range(2):
                    for k in range(KD):
                        mm = pe.matmul(PB[j % 2][0:r, a, :], sga[:, k, P * t:P * t + r], wo[a][:, k, :], start=(k == 0), stop=(k == KD - 1))
                mm.then_inc(S["proj_done"], 1)
                if t:
                    hf_turn(t - 1)
                if t >= 2:
                    route(t - 2)
            route(NTILE - 2)
            hf_turn(NTILE - 1)
            route(NTILE - 1)
            pe.wait_ge(S["m_ready"], 1)
            pe.matmul(bank(6, NE * NTILE), tri, rt_m.rearrange("p t e -> p (t e)"), start=True, stop=False)
            pe.matmul(bank(6, NE * NTILE), ones[:, :], rt_before[:, 0:NTILE, :].rearrange("p t e -> p (t e)"), start=False, stop=True)
            pe.matmul(bank(6, NE, NE * NTILE), ones[:, :], rt_before[:, NTILE, :], start=True, stop=True).then_inc(S["rank_ready"], 1)
            pe.wait_ge(S["gtr_ready"], 1)
            for t in range(4):
                pe.transpose(bank(7, P, P * t)[0:NE], rt_g[:, t, :], ident)
            pe.wait_ge(S["log_taken"], NTILE)
            pe.transpose(bank(5, P)[0:NE], rt_g[:, 4, :], ident).then_inc(S["gtr_ready"], 1)

            def pick(n, e, u):
                pe.wait_ge(S["cmp_ready"], n)
                for t in range(NTILE):
                    mm = pe.matmul(bank(6, 3, 8 * u)[0:CAP], cmpm[u][:, t, :], gx[:, t, bass.ds(e, 1), :].rearrange("p a x -> p (a x)"),
                                   start=(t == 0), stop=(t == NTILE - 1))
                mm.then_inc(S["slot_ready"], 1)

            def turn_rows(n, half, u):
                pe.wait_ge(gath[u], half * 16)
                for k in range(KD):
                    mm = pe.transpose(bank(2 + k // 4, CAP, CAP * (k % 4)), xg[u][0:CAP, P * k:P * k + P], ident[0:CAP, 0:CAP])
                mm.then_inc(S["xt_ready"], 1)

            def experts(b):
                pick(b * SELS + 1, 0, 0)
                turn_rows(b * SELS + 1, b * (NE // 2 + 1) + 1, 0)
                pe.wait_ge(S["gT_done"], 1)
                with pe.Fori(0, NE // 2) as i:
                    for u in range(2):
                        e = i * 2 + u
                        ne = b * NE + e
                        for c in range(CHUNKS):
                            pe.wait_ge(r_full[c], (ne + 1) * 16)
                            if c == 0:
                                pe.wait_ge(S["hTe_ready"], b * SELS + e + 1)
                            pe.wait_ge(S["gu_taken"], ne * CHUNKS + c + 1)
                            wc = W6[:, slot(c):slot(c + 1)].rearrange("p (k f x) -> p k f x", k=KD, f=4)
                            for f in range(4):
                                for k in range(KD):
                                    mm = pe.matmul(bank(c % 2, CAP, CAP * f), wc[:, k, f, :], hTe[:, k, :], start=(k == 0), stop=(k == KD - 1))
                            mm.then_inc(S["gu_ready"], 1)
                            if c == 1:
                                pick(b * SELS + e + 2, e + 1, 1 - u)
                        if u == 0:
                            turn_rows(b * SELS + e + 2, b * (NE // 2) + i + 1, 1)
                        else:
                            turn_rows(b * SELS + e + 2, b * (NE // 2 + 1) + i + 2, 0)
                        pe.wait_ge(S["y_ready"], ne + 1)
                        for f in range(KD):
                            if f % 2 == 0:
                                pe.wait_ge(S["act_ready"], ne * CHUNKS + f // 2 + 1)
                            pe.wait_ge(S["w_split"], ne * KD + f + 1)
                            for x, y in ((act_hi, w_hi), (act_hi, w_lo), (act_lo, w_hi)):
                                for a in range(2):
                                    mm = pe.matmul(PSF[0:CAP, (4 + a) * 512:(5 + a) * 512], x[:, f, :], y[:, f % 4, 512 * a:512 * a + 512],
                                                   start=(f == 0 and x is act_hi and y is w_hi), stop=(f == KD - 1 and x is act_lo))
                            mm.then_inc(S["part_used"], 1)

            pe.wait_ge(S["cnt_ready"], 1)
            pe.sem_inc(S["part_used"], 4)
            most = pe.value_load(cnt_i[0:1, 0:1], min_val=0, max_val=NT)
            experts(0)
            with pe.Fori(1, PASSES) as b:
                with pe.If(b * CAP < most):
                    experts(b)
            pe.wait_ge(S["all_added"], 1)
            pe.wait_ge(S["bd_in"], 16)
            pe.wait_ge(S["gT_done"], 1)
            for t in range(NTILE):
                if t >= 2:
                    pe.wait_ge(S["fin_gb"], t - 1)
                for a in range(2):
                    mm = pe.matmul(PB[t % 2][0:TROWS[t], a, :], gT[0:NE, t, 0:TROWS[t]], bd_sb[0:NE, 512 * a:512 * a + 512], start=True, stop=True)
                mm.then_inc(S["gb_ready"], 1)

        @block.vector
        def _(dve):
            n = [0]
            L = lambda ins: link(dve, ins, "dve_step", n)
            dve.memset(pT[:, :, 0:PAD], 0.0)
            dve.memset(pool_a[:, 0:PAD], 0.0)
            dve.memset(pool_b[:, 0:PAD], 0.0).then_inc(S["pool_pad"], 1)
            for hp in range(2):
                dve.memset(qi_v[hp][64 - 64 * hp:128 - 64 * hp], 0.0).then_inc(S["qi_zero"], 1)
            dve.wait_ge(S["act_taken"], 1)
            L(dve.reciprocal(KI[:, :], KI[:, :]))
            dve.wait_ge(S["gmix_in"], 16)
            for k in range(KD):
                dve.scalar_tensor_tensor(out=hT[:, k, :], in0=x_in[:, k, :], scalar=gmix_sb[:, k:k + 1], in1=KI[:, :],
                                         op0=ALU.mult, op1=ALU.mult).then_inc(S["h_done"], 1)
            dve.wait_ge(S["act_taken"], J_WI + 1)
            for i, (t, h) in enumerate(DOTS):
                dve.wait_ge(S["relu_done"], i + 1)
                r, w = ROWS[t], KEYS[t]
                sc = score[0:r, SCORE_AT[t]:SCORE_AT[t] + w]
                rl = relu_p[i % 2][0:r, 0:w]
                if h == 0:
                    dve.tensor_scalar(sc, rl, wi_nat[0:r, t, h:h + 1], None, ALU.mult).then_inc(S["acc_done"], 1)
                else:
                    dve.wait_ge(S["acc_done"], i)
                    dve.scalar_tensor_tensor(out=sc, in0=rl, scalar=wi_nat[0:r, t, h:h + 1], in1=sc,
                                             op0=ALU.mult, op1=ALU.add).then_inc(S["acc_done"], 1)
            dve.wait_ge(S["dots_ready"], len(DOTS) + 2)
            dve.tensor_copy(score_s[0:NS], PSF[0:NS, 4 * 512:4 * 512 + KEYS_S]).then_inc(S["sidx_taken"], 1)
            dve.wait_ge(S["sidx_taken"], 1)

            def top(sc, rows, k):
                for _ in range(k // 8):
                    L(dve.max(out=max8[0:rows], in_=sc))
                    L(dve.match_replace(out=sc, in_to_replace=max8[0:rows], in_values=sc, imm_value=TAKEN))
            top(score_s[0:NS], NS, TOPK_S)
            dve.tensor_scalar(score_s[0:NS], score_s[0:NS], (NONCAUSAL + TAKEN) / 2, OUT, ALU.is_gt, ALU.mult).then_inc(S["smask_done"], 1)
            dve.wait_ge(S["Lqk_done"], 1)
            dve.wait_ge(S["slot5_set"], 1)
            dve.wait_ge(S["bias_in"], 16)
            dve.wait_ge(S["small_in"], 96)
            for g in range(2):
                L(dve.tensor_tensor(lg_s[:, g, 0:256], L_g[g], bias_sb, ALU.add))
                L(dve.tensor_scalar(lg_s[0:32, g, 256:257], L_n[g], bias_new[0:32], None, ALU.add))
            dve.tensor_reduce(mx2, lg_s, AX.X, ALU.max).then_inc(S["lgs_done"], 1)
            dve.wait_ge(S["mxT_ready"], 1)
            L(dve.tensor_reduce(mq, bank(7, P)[0:2].rearrange("g (j x) -> g x j", j=4), AX.X, ALU.max))
            dve.tensor_scalar(mq4.rearrange("g (j x) -> g j x", j=4), mq.unsqueeze(1).broadcast_to([2, 4, 32]), -1.0, None, ALU.mult)\
                .then_inc(S["mq_done"], 1)
            dve.wait_ge(S["mb_ready"], 1)
            dve.tensor_copy(nmx2, bank(7, 2, P)).then_inc(S["nmax_s"], 1)

            def top_tile(t):
                r, w = ROWS[t], KEYS[t]
                sc = score[0:r, SCORE_AT[t]:SCORE_AT[t] + w]
                dve.wait_ge(S["causal_done"], 5 - t)
                top(sc, r, TOPK_P)
                dve.tensor_scalar(sc, sc, (NONCAUSAL + TAKEN) / 2, OUT, ALU.is_gt, ALU.mult).then_inc(S["mask_done"], 1)
            top_tile(1)
            dve.wait_ge(S["sums_ready"], 1)
            L(dve.reciprocal(rs2, bank(7, 2, 132)))
            for g in range(2):
                dve.tensor_scalar(lg_s[:, g, :], lg_s[:, g, :], rs2[:, g:g + 1], None, ALU.mult).then_inc(S["ps_norm"], 1)
            dve.wait_ge(S["ps_norm"], 2)
            for g in range(2):
                ins = dve.tensor_scalar(dnew[:, g, :], ident[0:32, 0:32], lg_s[0:32, g, 256:257], None, ALU.mult)
            ins.then_inc(S["ptz_done"], 1)
            dve.wait_ge(S["psT_ready"], 1)
            for m in range(4):
                ins = dve.tensor_copy(ptz[:, :, 40 * m:40 * m + 8], bank(7).rearrange("p (q x) -> p q x", x=32)[:, :, 8 * m:8 * m + 8])
            ins.then_inc(S["ptz_done"], 1)
            for t in (2, 3, 4):
                top_tile(t)
            for g in range(2):
                dve.wait_ge(S["og_ready"], g + 1)
                dve.tensor_tensor(om[:, g, :].rearrange("p (h d) -> p h d", h=H), O_g[g].rearrange("p (h d) -> p h d", h=H),
                                  head8.unsqueeze(2).broadcast_to([P, H, HD]), ALU.mult).then_inc(S["om_done"], 1)
            dve.wait_ge(S["act_taken"], J_A)
            for g in range(2):
                dve.wait_ge(S["as_ready"], g + 1)
                dve.tensor_copy(attnT[:, :, NP_ + 4 * g:NP_ + 4 * g + 4], bank(7 - 3 * g, 16).rearrange("p (c m) -> p c m", c=4))\
                    .then_inc(S["attn_s_done"], 1)
            def normalise(i):
                t, h = HEADS[i]
                p = lg[i % 4][0:ROWS[t], 0:KEYS[t]]
                dve.wait_ge(S["exp_done"], i + 1)
                L(dve.reciprocal(rsum[0:ROWS[t], i:i + 1], esum[0:ROWS[t], i:i + 1]))
                dve.tensor_scalar(p, p, rsum[0:ROWS[t], i:i + 1], None, ALU.mult).then_inc(S["p_norm"], 1)
            for i, (t, h) in enumerate(HEADS):
                r, w = ROWS[t], KEYS[t]
                dve.wait_ge(S["s_ready"], i + 1)
                dve.wait_ge(S["mb_done"], i + 1)
                if i >= 4:
                    dve.wait_ge(S["pt_ready"], i - 3)
                dve.tensor_tensor_reduce(lg[i % 4][0:r, 0:w], SB_[i % 2][0:r, 0:w], mb[i % 2][0:r, 0:w], -1.0, 3.0e38,
                                         ALU.add, ALU.min, nmax[0:r, i:i + 1]).then_inc(S["lgp_done"], 1)
                if i:
                    normalise(i - 1)
            normalise(len(HEADS) - 1)
            dve.wait_ge(S["b_mult"], KD)
            for d in range(KD):
                j = J_A + d
                dve.wait_ge(S["proj_done"], j + 1)
                m = sga[:, d, :].rearrange("p (a b) -> p a b", a=2)
                dve.tensor_tensor(m, PB[j % 2][:, :, 0:HALF], m, ALU.mult).then_inc(S["dve_taken"], 1)
                dve.wait_ge(S["dve_taken"], d + 1)
                dve.tensor_tensor(sga[:, d, :], sga[:, d, :], sbb[:, d, :], ALU.add).then_inc(S["m_done"], 1)
            def norm_rows(t):
                r = TROWS[t]
                dve.wait_ge(S["row_ms"], 2 * t + 2)
                L(dve.reciprocal(rms[0:r, t:t + 1], rms[0:r, t:t + 1]))
                dve.scalar_tensor_tensor(out=hf(t)[0:r], in0=xn(t)[0:r], scalar=rms[0:r, t:t + 1], in1=gffn[0:r],
                                         op0=ALU.mult, op1=ALU.mult).then_inc(S["hf_done"], 1)
            def find(t):
                r = TROWS[t]
                dve.wait_ge(S["router_ready"], t + 1)
                dve.tensor_tensor(rt_log[0:r, t, :], bank(4 + t % 2, NE)[0:r], rt_br[0:r], ALU.add).then_inc(S["log_taken"], 1)
                dve.wait_ge(S["log_taken"], t + 1)
                L(dve.max(out=top_v[:, t, :], in_=rt_log[:, t, :]))
                L(dve.max_index(out=top_i[:, t, :], in_max=top_v[:, t, :], in_values=rt_log[:, t, :]))
            dve.wait_ge(S["xn_in"], 16 * NTILE)
            for t in range(NTILE):
                j, r = J_WO + t, TROWS[t]
                dve.wait_ge(S["proj_done"], j + 1)
                x1 = xn(t)[0:r].rearrange("p (a b) -> p a b", a=2)
                dve.tensor_tensor(x1, PB[j % 2][0:r], x1, ALU.add).then_inc(S["dve_taken"], 1)
                if t == 0:
                    dve.wait_ge(S["late_in"], 48)
                    L(dve.memset(rt_log, 0.0))
                    L(dve.memset(posv, -1.0))
                    L(dve.memset(gx, 0.0))
                    L(dve.tensor_copy(gx[:, :, 0:NE, 0], tokid.unsqueeze(2).broadcast_to([P, NTILE, NE])))
                    L(dve.memset(gx[:, :, 0:NE, 1], 1.0))
                norm_rows(t)
                if t >= 2:
                    find(t - 2)
            find(NTILE - 2)
            find(NTILE - 1)
            L(dve.tensor_copy(rt_e, top_i[:, :, :]))
            dve.tensor_tensor(rt_w, top_v[:, :, 0:TOPE], top_v[:, :, 0:1].broadcast_to([P, NTILE, TOPE]), ALU.subtract).then_inc(S["sel_ready"], 1)
            L(dve.tensor_tensor(rt_eq, iota_e.unsqueeze(1).unsqueeze(1).broadcast_to([P, NTILE, TOPE, NE]),
                                rt_e[:, :, 0:TOPE].unsqueeze(3).broadcast_to([P, NTILE, TOPE, NE]), ALU.is_equal))
            L(dve.tensor_reduce(rt_m, rt_eq.rearrange("p t k e -> p t e k"), AX.X, ALU.add))
            L(dve.tensor_tensor(rt_m[:, 4, :], rt_m[:, 4, :], valid.broadcast_to([P, NE]), ALU.mult))
            L(dve.memset(rt_before[:, 0, :], 0.0))
            for t in range(NTILE):
                ins = dve.tensor_tensor(rt_before[:, t + 1, :], rt_before[:, t, :], rt_m[:, t, :], ALU.add)
                if t < NTILE - 1:
                    L(ins)
            ins.then_inc(S["m_ready"], 1)
            dve.wait_ge(S["sel_ready"], 2)
            L(dve.tensor_reduce(sum4, rt_w, AX.X, ALU.add))
            L(dve.reciprocal(sum4, sum4))
            L(dve.tensor_tensor(rt_w, rt_w, sum4.unsqueeze(2).broadcast_to([P, NTILE, TOPE]), ALU.mult))
            L(dve.tensor_tensor(rt_eg, rt_eq, rt_w.unsqueeze(3).broadcast_to([P, NTILE, TOPE, NE]), ALU.mult))
            dve.tensor_reduce(rt_g, rt_eg.rearrange("p t k e -> p t e k"), AX.X, ALU.add).then_inc(S["gtr_ready"], 1)
            dve.wait_ge(S["gtr_ready"], 1)
            L(dve.tensor_copy(gx[:, :, 0:NE, 2], rt_g))
            dve.wait_ge(S["m_ready"], 1)
            dve.wait_ge(S["rank_ready"], 1)
            L(dve.scalar_tensor_tensor(out=rt_eg[:, :, 0, :], in0=bank(6, NTILE * NE).rearrange("p (t e) -> p t e", t=NTILE), scalar=1.0, in1=rt_m,
                                       op0=ALU.add, op1=ALU.mult))
            L(dve.tensor_scalar(posv[:, :, 0:NE], rt_eg[:, :, 0, :], -1.0, None, ALU.add))
            L(dve.tensor_reduce(rt_cnt[0:1, 0:1], bank(6, NE, NE * NTILE)[0:1], AX.X, ALU.max))
            L(dve.tensor_copy(cnt_i[0:1, 0:1], rt_cnt[0:1, 0:1]))
            L(dve.tensor_copy(iota_b[:, :], iota96))
            dve.sem_inc(S["cnt_ready"], 1)
            dve.wait_ge(S["gtr_ready"], 2)
            dve.wait_ge(S["hfT_ready"], NTILE)
            dve.wait_ge(S["acc_init"], 16 * 2 * NTILE)
            L(dve.tensor_copy(gT[0:NE, 0:4, :], bank(7)[0:NE].rearrange("p (t x) -> p t x", t=4)))
            dve.tensor_copy(gT[0:NE, 4, :], bank(5, P)[0:NE]).then_inc(S["gT_done"], 1)
            dve.wait_ge(S["bgu_in"], 16)
            dve.sem_inc(S["gu_taken"], 2)

            def compare(e, u):
                dve.tensor_tensor(cmpm[u], iota_b[:, :].unsqueeze(1).broadcast_to([P, NTILE, CAP]),
                                  posv[:, :, bass.ds(e, 1)].broadcast_to([P, NTILE, CAP]), ALU.is_equal).then_inc(S["cmp_ready"], 1)

            def index(nsel, u):
                dve.wait_ge(S["slot_ready"], nsel)
                sl = bank(6, 3, 8 * u)[0:CAP]
                dve.scalar_tensor_tensor(out=unused[u][0:CAP], in0=trash[0:CAP], scalar=sl[:, 1:2], in1=trash[0:CAP], op0=ALU.mult, op1=ALU.subtract)\
                    .then_inc(S["unused_done"], 1)
                dve.wait_ge(S["unused_done"], nsel)
                dve.tensor_tensor(idx_i[u][0:CAP, :], sl[:, 0:1], unused[u][0:CAP], ALU.subtract)
                dve.tensor_copy(gcol[u][0:CAP], sl[:, 2:3]).then_inc(S["idx_ready"], 1)

            def low(ne, f):
                dve.wait_ge(S["w_high"], ne * KD + f + 1)
                dve.tensor_tensor(w_lo[:, f % 4, :], W6[:, slot(4) + D * f:slot(4) + D * f + D], w_hi[:, f % 4, :].bitcast(F32), ALU.subtract)\
                    .then_inc(S["w_split"], 1)

            def experts(b):
                compare(0, 0)
                index(b * SELS + 1, 0)
                with dve.Fori(0, NE // 2) as i:
                    for u in range(2):
                        e = i * 2 + u
                        ne = b * NE + e
                        compare(e + 1, 1 - u)
                        for c in range(CHUNKS):
                            nc_ = ne * CHUNKS + c
                            if c == 2:
                                if u == 0:
                                    dve.wait_ge(scat[1], (b * (NE // 2) + i + 1) * 16)
                                else:
                                    dve.wait_ge(scat[0], (b * (NE // 2) + i + 2) * 16)
                                index(b * SELS + e + 2, 1 - u)
                            dve.wait_ge(S["gu_ready"], nc_ + 1)
                            t_ = gu_t[c % 2]
                            dve.tensor_tensor(t_, bank(c % 2, 4 * CAP).rearrange("p (f s) -> p f s", f=4),
                                              b_gu_sb[:, bass.ds(e, 1), 4 * c:4 * c + 4].rearrange("p a f -> p (a f)").unsqueeze(2).broadcast_to([P, 4, CAP]),
                                              ALU.add).then_inc(S["gu_taken"], 1)
                            dve.wait_ge(S["gu_taken"], nc_ + 3)
                            dve.tensor_scalar(t_[:, 0:2, :], t_[:, 0:2, :], 7.0, None, ALU.min).then_inc(S["clamp_done"], 1)
                            dve.tensor_scalar(t_[:, 2:4, :], t_[:, 2:4, :], 7.0, -7.0, ALU.min, ALU.max).then_inc(S["up_done"], 1)
                            dve.wait_ge(S["clamp_done"], nc_ + 1)
                            dve.wait_ge(S["sig_done"], nc_ + 1)
                            dve.tensor_tensor(gs_t, t_[:, 0:2, :], sg_t[c % 2], ALU.mult).then_inc(S["gated"], 1)
                            dve.wait_ge(S["up_done"], nc_ + 1)
                            dve.wait_ge(S["gated"], nc_ + 1)
                            dve.scalar_tensor_tensor(out=act_t, in0=t_[:, 2:4, :], scalar=1.0, in1=gs_t,
                                                     op0=ALU.add, op1=ALU.mult).then_inc(S["act_done"], 1)
                            dve.wait_ge(S["act_done"], nc_ + 1)
                            dve.tensor_copy(act_hi[:, 2 * c:2 * c + 2, :], act_t).then_inc(S["act_high"], 1)
                            dve.wait_ge(S["act_high"], nc_ + 1)
                            dve.tensor_tensor(act_lo[:, 2 * c:2 * c + 2, :], act_t, act_hi[:, 2 * c:2 * c + 2, :].bitcast(F32), ALU.subtract)\
                                .then_inc(S["act_ready"], 1)
                            low(ne, c)
                        for f in range(CHUNKS, KD):
                            low(ne, f)

            most = dve.value_load(cnt_i[0:1, 0:1], min_val=0, max_val=NT)
            experts(0)
            with dve.Fori(1, PASSES) as b:
                with dve.If(b * CAP < most):
                    dve.tensor_scalar(iota_b[:, :], iota_b[:, :], float(CAP), None, ALU.add).then_inc(S["slots_moved"], 1)
                    dve.wait_ge(S["slots_moved"], b)
                    experts(b)
            def fin_row(t):
                r = TROWS[t]
                dve.wait_ge(S["fin_rs"], t + 1)
                L(dve.reciprocal(rms2[0:r, t:t + 1], rms2[0:r, t:t + 1]))
                dve.scalar_tensor_tensor(out=yf[0:r, t, :], in0=yf[0:r, t, :], scalar=rms2[0:r, t:t + 1], in1=gfin[0:r],
                                         op0=ALU.mult, op1=ALU.mult).then_inc(S["fin_y"], 1)
            for t in range(NTILE):
                r = TROWS[t]
                dve.wait_ge(yf_full[t], 16)
                dve.wait_ge(S["gb_ready"], t + 1)
                y2 = yf[0:r, t, :].rearrange("p (a b) -> p a b", a=2)
                dve.tensor_tensor(y2, PB[t % 2][0:r], y2, ALU.add).then_inc(S["fin_gb"], 1)
                if t:
                    fin_row(t - 1)
            fin_row(NTILE - 1)


def constants():
    c = np.zeros((P, C_W), np.float32)
    i = np.arange(P)
    c[:, C_ID:C_ID + P] = np.eye(P)
    c[:, C_TRI:C_TRI + P] = i[:, None] < i[None, :]
    c[:, C_IOTA:C_IOTA + CAP] = np.arange(CAP)
    c[:, C_EXP:C_EXP + NE] = np.arange(NE)
    c[:, C_TOK:C_TOK + NTILE] = i[:, None] + P * np.arange(NTILE)
    c[:, C_TRASH] = NT + i
    for g in range(PG):
        c[:, C_RCNT + 16 * g:C_RCNT + 16 * g + 16] = 1.0 / np.minimum(np.arange(16) + 1, 2 << g)
    c[:, C_WSEL:C_WSEL + NS] = i[:, None] // H == np.arange(NS)
    c[:, C_VALID] = i < TAIL
    for g in range(2):
        c[:NS, C_SELG + 32 * g:C_SELG + 32 * g + 32] = i[:NS, None] == 4 * g + np.arange(32) // H
    c[:, C_G32:C_G32 + P] = i[:, None] % 32 == i[None, :] % 32
    c[:, C_SELM:C_SELM + 4] = i[:, None] % 32 // H == np.arange(4)
    c[:, C_H8:C_H8 + H] = i[:, None] % H == np.arange(H)
    return c


def buckets(dist):
    n = np.maximum(dist, 0)
    exact = NB // 2
    large = exact + (np.log(np.maximum(n, 1) / exact) / np.log(128 / exact) * (NB - exact)).astype(np.int64)
    return np.where(n < exact, n, np.minimum(large, NB - 1))


def kernel(**inputs):
    import concourse.bacc as bacc
    from concourse.bass_utils import run_bass_kernel_spmd

    x = {k: np.asarray(v) for k, v in inputs.items()}
    rows = np.concatenate([x["meta_tokens"], x["x_prompt"][0], x["x_sample"][:, 0]], axis=0)
    w_in = x["w_in"][0]
    q, k, v, qi, ki, wi, p, ga, gb = np.split(w_in, np.cumsum([AW, AW, AW, AW, HD, H, AW, D, D])[:-1], axis=1)

    def tiles(w):
        return w.reshape(KD, P, -1, P).transpose(2, 1, 0, 3)
    gates = np.stack([tiles(gb), tiles(ga)], axis=1).reshape(2 * KD, P, KD, P)
    w_mt = np.concatenate([tiles(qi), tiles(np.concatenate([ki, ki], axis=1)), tiles(k), tiles(q), tiles(p), gates])

    def rows4(w):
        return w.reshape(4, P, KD, P).transpose(2, 1, 0, 3).reshape(KD, P, 512)
    i = np.arange(P)
    strip = x["rel_bias"][buckets(512 + i[:, None] - np.arange(STRIP)[None, :])].transpose(0, 2, 1)
    dist = PAST - (256 * (i[:, None] // 32) + np.arange(256)[None, :])
    arrays = {
        "xT": rows.T.reshape(KD, P, NT).transpose(1, 0, 2),
        "xnat": rows,
        "consts": constants(),
        "g_mix": x["g_mix"][0].reshape(KD, P).T,
        "w_mt": w_mt.reshape(-1, P, KD * P),
        "w_wi": wi.reshape(KD, P, H).transpose(1, 0, 2),
        "w_v": v.reshape(KD, P, AW).transpose(1, 0, 2),
        "w_mix": x["w_pool_mix"][0].transpose(1, 0, 2),
        "pool_scale": x["pool_scale"][0].reshape(PG, P).T,
        "w_bra": rows4(x["w_br_attn"][0]),
        "w_brp": rows4(x["w_br_pool"][0]),
        "w_out": x["w_out"][0].reshape(KD, P, 2, 512).transpose(2, 1, 0, 3),
        "w_router": x["w_router"][0].reshape(KD, P, NE).transpose(1, 0, 2),
        "b_router": x["b_router"][0],
        "b_gu": x["b_gate_up"][0].reshape(NE, 2, CHUNKS, 2, P).transpose(4, 0, 2, 1, 3).reshape(P, NE, 16),
        "w_gu": x["w_gate_up"][0].reshape(NE, KD, P, 2, CHUNKS, 2, P).transpose(0, 4, 2, 1, 3, 5, 6).reshape(NE, CHUNKS, P, RING),
        "w_down": x["w_down"][0].reshape(NE, 2, 4, P, D).transpose(0, 1, 3, 2, 4).reshape(NE, 2, P, RING),
        "b_down": x["b_down"][0],
        "g_ffn": x["g_ffn"][0],
        "g_final": x["g_final"],
        "bias_strip": strip,
        "bias_s": x["rel_bias"][buckets(dist), i[:, None] % H],
        "bias_n": x["rel_bias"][0, i[:, None] % H],
        "cache_kT": x["cache_k"][0].reshape(NPOOL, PAGE, 4, P).transpose(0, 3, 2, 1).reshape(NPOOL, P, 4 * PAGE),
        "cache_v": x["cache_v"][0].reshape(NPOOL, PAGE, AW),
        "cache_kiT": x["cache_kidx"][0].transpose(0, 2, 1),
        "page_table": x["page_table"].reshape(1, NS * NPAGE),
        "state": x["state_pool"][0],
        "stateT": x["state_pool"][0].reshape(NS, 15, PG, P).transpose(3, 2, 0, 1).reshape(P, PG * NS, 15),
    }
    outs = [("o_y", (NT, D)), ("o_kT", (P, 4, NT)), ("o_v", (NT, AW)), ("o_kiT", (HD, NT)), ("o_pT", (P, PG, 23)),
            ("o_state", (NS, 14, AW))]
    nc = bacc.Bacc("TRN2", target_bir_lowering=False, num_devices=1)
    args, feed = [], {}
    for name, a in arrays.items():
        a = np.ascontiguousarray(a)
        feed[name] = a
        args.append(nc.dram_tensor(name, a.shape, mybir.dt.from_np(a.dtype), kind="ExternalInput").ap())
    for name, shape in outs:
        args.append(nc.dram_tensor(name, shape, F32, kind="ExternalOutput").ap())
    build_step(nc, *args)
    r = run_bass_kernel_spmd(nc, [feed], core_ids=[0]).results[0]
    y = r["o_y"]
    kk = r["o_kT"].transpose(2, 1, 0).reshape(NT, H, HD)
    vv = r["o_v"].reshape(NT, H, HD)
    kki = r["o_kiT"].T
    pp = r["o_pT"].transpose(2, 1, 0).reshape(23, AW)
    new_pool = np.concatenate([r["o_state"], pp[15:, None]], axis=1)
    return (y[META:NP_][None], y[NP_:][:, None], kk[:NP_][None, None], vv[:NP_][None, None], kki[:NP_][None, None],
            pp[:15][None, None], kk[NP_:][None, :, None], vv[NP_:][None, :, None], kki[NP_:][None, :, None], new_pool[None])
```
